# Optimizing a Trainium2 kernel written in Bass

```python
import jax, jax.numpy as jnp
from jax import lax
import numpy as np

D_MODEL = 1024
BATCH = 1
SEQ = 2048
DEPTH = 2

CHUNK = 64
N_MIXERS = 2
N_ATTN_LAYERS = (DEPTH + 1) // 2
N_RNN_LAYERS = DEPTH // 2

ATTN_HEADS = 16
ATTN_HEAD_DIM = D_MODEL // ATTN_HEADS
ATTN_WIDTH = ATTN_HEADS * ATTN_HEAD_DIM
Q_BLOCK = 128

RNN_WIDTH = D_MODEL
RNN_BLOCK_WIDTH = 256
RNN_BLOCKS = RNN_WIDTH // RNN_BLOCK_WIDTH
CONV_WIDTH = 4
LRU_C = 8.0

DEEPNORM_ALPHA = (2.0 * DEPTH) ** 0.25
DEEPNORM_BETA = (8.0 * DEPTH) ** -0.25
LN_EPS = 1e-5

kernel_name = "fox_rglru_deepnorm_hybrid"

def layer_norm(x, g, b):
    xf = x.astype(jnp.float32)
    mu = jnp.mean(xf, axis=-1, keepdims=True)
    var = jnp.mean(jnp.square(xf - mu), axis=-1, keepdims=True)
    y = (xf - mu) * lax.rsqrt(var + LN_EPS) * g.astype(jnp.float32) + b.astype(jnp.float32)
    return y.astype(x.dtype)

def forgetting_attention(x, w_in, b_f, w_out):
    B, S, _ = x.shape
    H, Dh = ATTN_HEADS, ATTN_HEAD_DIM
    proj = jnp.einsum("bsd,de->bse", x, w_in)
    q, k, v, gate = jnp.split(proj[..., :4 * ATTN_WIDTH], 4, axis=-1)
    f_logit = proj[..., 4 * ATTN_WIDTH:].astype(jnp.float32) + b_f.astype(jnp.float32)
    cum = jnp.cumsum(jax.nn.log_sigmoid(f_logit), axis=1).transpose(0, 2, 1)

    def heads(t):
        return t.reshape(B, S, H, Dh).transpose(0, 2, 1, 3)

    q = heads(q) * (Dh ** -0.5)
    k = heads(k)
    v = heads(v)
    outs = []
    for blk in range(S // Q_BLOCK):
        q0 = blk * Q_BLOCK
        q1 = q0 + Q_BLOCK
        s = jnp.einsum("bhqd,bhkd->bhqk", q[:, :, q0:q1], k[:, :, :q1]).astype(jnp.float32)
        s = s + cum[:, :, q0:q1, None] - cum[:, :, None, :q1]
        causal = (q0 + jnp.arange(Q_BLOCK))[:, None] >= jnp.arange(q1)[None, :]
        p = jax.nn.softmax(jnp.where(causal, s, -jnp.inf), axis=-1)
        outs.append(jnp.einsum("bhqk,bhkd->bhqd", p.astype(v.dtype), v[:, :, :q1]))
    o = jnp.concatenate(outs, axis=2).transpose(0, 2, 1, 3).reshape(B, S, ATTN_WIDTH)
    return jnp.einsum("bse,ed->bsd", o * jax.nn.silu(gate), w_out)

def rglru_block(x, w_in, conv_w, conv_b, w_a, b_a, w_i, b_i, lam, w_out):
    B, S, _ = x.shape
    proj = jnp.einsum("bsd,de->bse", x, w_in)
    u, gate = jnp.split(proj, 2, axis=-1)
    u_pad = jnp.pad(u, ((0, 0), (CONV_WIDTH - 1, 0), (0, 0)))
    u = conv_b + sum(u_pad[:, tap:tap + S] * conv_w[tap] for tap in range(CONV_WIDTH))
    ub = u.reshape(B, S, RNN_BLOCKS, RNN_BLOCK_WIDTH)
    r = jax.nn.sigmoid(jnp.einsum("bsnc,ncd->bsnd", ub, w_a).reshape(B, S, RNN_WIDTH) + b_a)
    i = jax.nn.sigmoid(jnp.einsum("bsnc,ncd->bsnd", ub, w_i).reshape(B, S, RNN_WIDTH) + b_i)
    log_a = -LRU_C * r.astype(jnp.float32) * jax.nn.softplus(-lam.astype(jnp.float32))
    a = jnp.exp(log_a)
    bterm = jnp.sqrt(-jnp.expm1(2.0 * log_a)) * (i * u).astype(jnp.float32)

    def combine(left, right):
        a1, b1 = left
        a2, b2 = right
        return a1 * a2, a2 * b1 + b2

    _, h = lax.associative_scan(combine, (a, bterm), axis=1)
    y = h.astype(x.dtype) * jax.nn.silu(gate)
    return jnp.einsum("bse,ed->bsd", y, w_out)

def setup_inputs(seed: int = 0) -> dict:
    key = jax.random.key(seed)
    ks = jax.random.split(key, 16)
    nA, nR = N_ATTN_LAYERS, N_RNN_LAYERS
    f32 = jnp.float32
    x = jax.random.normal(ks[0], (BATCH, SEQ, D_MODEL), f32)
    ln_g = 1.0 + 0.02 * jax.random.normal(ks[1], (DEPTH, D_MODEL), f32)
    ln_b = 0.02 * jax.random.normal(ks[2], (DEPTH, D_MODEL), f32)
    attn_w_in = jax.random.normal(ks[3], (nA, D_MODEL, 4 * ATTN_WIDTH + ATTN_HEADS), f32) * D_MODEL ** -0.5
    attn_b_f = jax.random.uniform(ks[4], (nA, ATTN_HEADS), f32, 1.0, 4.0)
    attn_w_out = jax.random.normal(ks[5], (nA, ATTN_WIDTH, D_MODEL), f32) * (ATTN_WIDTH ** -0.5 * DEEPNORM_BETA)
    rnn_w_in = jax.random.normal(ks[6], (nR, D_MODEL, 2 * RNN_WIDTH), f32) * D_MODEL ** -0.5
    rnn_conv_w = jax.random.normal(ks[7], (nR, CONV_WIDTH, RNN_WIDTH), f32) * CONV_WIDTH ** -0.5
    rnn_conv_b = 0.02 * jax.random.normal(ks[8], (nR, RNN_WIDTH), f32)
    rnn_w_a = jax.random.normal(ks[9], (nR, RNN_BLOCKS, RNN_BLOCK_WIDTH, RNN_BLOCK_WIDTH), f32) * RNN_BLOCK_WIDTH ** -0.5
    rnn_b_a = 0.02 * jax.random.normal(ks[10], (nR, RNN_WIDTH), f32)
    rnn_w_i = jax.random.normal(ks[11], (nR, RNN_BLOCKS, RNN_BLOCK_WIDTH, RNN_BLOCK_WIDTH), f32) * RNN_BLOCK_WIDTH ** -0.5
    rnn_b_i = 0.02 * jax.random.normal(ks[12], (nR, RNN_WIDTH), f32)
    a0 = jax.random.uniform(ks[13], (nR, RNN_WIDTH), f32, 0.9, 0.999)
    rnn_lambda = jnp.log(a0) - jnp.log1p(-a0)
    rnn_w_out = jax.random.normal(ks[14], (nR, RNN_WIDTH, D_MODEL), f32) * (RNN_WIDTH ** -0.5 * DEEPNORM_BETA)
    return {
        "x": x, "ln_g": ln_g, "ln_b": ln_b,
        "attn_w_in": attn_w_in, "attn_b_f": attn_b_f, "attn_w_out": attn_w_out,
        "rnn_w_in": rnn_w_in, "rnn_conv_w": rnn_conv_w, "rnn_conv_b": rnn_conv_b,
        "rnn_w_a": rnn_w_a, "rnn_b_a": rnn_b_a, "rnn_w_i": rnn_w_i, "rnn_b_i": rnn_b_i,
        "rnn_lambda": rnn_lambda, "rnn_w_out": rnn_w_out,
    }

def reference(x, ln_g, ln_b, attn_w_in, attn_b_f, attn_w_out, rnn_w_in, rnn_conv_w,
              rnn_conv_b, rnn_w_a, rnn_b_a, rnn_w_i, rnn_b_i, rnn_lambda, rnn_w_out):
    for layer in range(DEPTH):
        idx = layer // N_MIXERS
        if layer % N_MIXERS == 0:
            h = forgetting_attention(x, attn_w_in[idx], attn_b_f[idx], attn_w_out[idx])
        else:
            h = rglru_block(x, rnn_w_in[idx], rnn_conv_w[idx], rnn_conv_b[idx],
                            rnn_w_a[idx], rnn_b_a[idx], rnn_w_i[idx], rnn_b_i[idx],
                            rnn_lambda[idx], rnn_w_out[idx])
        x = layer_norm(DEEPNORM_ALPHA * x + h, ln_g[layer], ln_b[layer])
    return x


_drawn_inputs = setup_inputs


def setup_inputs(seed=0):
    import zlib

    import numpy as np

    out = dict(_drawn_inputs(seed))
    spreads = {}
    factors = {'rnn_conv_b': 5.87, 'rnn_b_a': 64.0, 'rnn_b_i': 55.859}
    for name, (base, spread) in spreads.items():
        noise = np.random.default_rng([zlib.crc32(name.encode()), seed]).standard_normal(out[name].shape)
        drawn = base * np.exp(spread * noise) if base else spread * noise
        out[name] = __import__('jax').numpy.asarray(drawn.astype(out[name].dtype))
    for name, factor in factors.items():
        out[name] = (out[name] * factor).astype(out[name].dtype)
    return out
```

```python
from contextlib import ExitStack

import concourse.bass as bass
from concourse import mybir

P = 128
BANK = 512
ALU = mybir.AluOpType
ACT = mybir.ActivationFunctionType
F32 = mybir.dt.float32
F32R = mybir.dt.float32r
BF16 = mybir.dt.bfloat16
AX_X = mybir.AxisListType.X

HEADS = 16
HEAD_DIM = 64
CONV_WIDTH = 4
LRU_C = 8.0
LN_EPS = 1e-5
ALPHA = (2.0 * 2) ** 0.25
STRIP = 256
MASKED = 1e30


class Alloc:

    def __init__(self, nc, ctx, stage):
        self.nc, self.ctx, self.stage = nc, ctx, stage

    def sb(self, name, shape, dt=F32):
        return self.ctx.enter_context(self.nc.sbuf_tensor(f"{self.stage}_{name}", shape, dt))

    def ps(self, name, shape, dt=F32):
        return self.ctx.enter_context(self.nc.psum_tensor(f"{self.stage}_{name}", shape, dt))

    def sem(self, name):
        return self.nc.alloc_semaphore(f"{self.stage}_{name}")


def raw(ap):
    return ap.bitcast(F32)


def project(nc, stage, x, w, groups, gate_bias=None, cum=None):
    S, D = x.shape
    KC = D // P
    ST = S // P
    NS = S // BANK
    TILES = 8
    RING = 4
    w_v = w.rearrange("(c p) f -> p c f", p=P)
    with ExitStack() as ctx:
        a = Alloc(nc, ctx, stage)
        xh = a.sb("xh", [P, KC, S], F32R)
        xl = a.sb("xl", [P, KC, S], F32R)
        fbuf = a.sb("fbuf", [P, S])
        fsm = a.sb("fsm", [HEADS, 3, BANK])
        wst = a.sb("wst", [P, 2, KC, STRIP])
        wh = a.sb("wh", [P, 2, KC, STRIP], F32R)
        wl = a.sb("wl", [P, 2, KC, STRIP], F32R)
        stg = a.sb("stg", [P, RING, 2, BANK], F32R)
        ident = a.sb("ident", [P, P])
        bf = a.sb("bf", [HEADS, 1])
        last = a.sb("last", [HEADS, 2])
        psum = [a.ps(f"ps{i}", [P, BANK]) for i in range(RING)]
        tps = [a.ps(f"tps{i}", [P, 4, P]) for i in range(4)]

        x_loaded = [a.sem(f"x_loaded{i}") for i in range(RING)]
        w_loaded = [a.sem(f"w_loaded{i}") for i in range(2)]
        stored = [a.sem(f"stored{i}") for i in range(RING)]
        ident_ready = a.sem("ident_ready")
        x_turned = a.sem("x_turned")
        high_out = a.sem("high_out")
        low_out = a.sem("low_out")
        w_split = a.sem("w_split")
        w_high = a.sem("w_high")
        products = a.sem("products")
        evac_h = a.sem("evac_h")
        evac_l = a.sem("evac_l")
        if cum is not None:
            f_in, f_zero, f_prod, f_act, f_dve, f_scan, f_split, f_stored = (
                a.sem(n) for n in ("f_in", "f_zero", "f_prod", "f_act", "f_dve", "f_scan", "f_split", "f_stored"))

        total_strips = sum(n for _, _, n, _ in groups)
        first_strip, t = [], 0
        for _, _, n, _ in groups:
            first_strip.append(t)
            t += n
        xin = [raw(stg[:, i, :, :]).rearrange("p a b -> p (a b)") for i in range(RING)]
        fz = [fbuf[0:HEADS, n * BANK:(n + 1) * BANK] for n in range(NS)]
        f_out = [[fbuf[32 * k:32 * k + HEADS, n * BANK:(n + 1) * BANK] for k in range(4)] for n in range(NS)]
        fe, fo, fcum = (fsm[:, k, :] for k in range(3))
        wfs = wst[:, 1, :, 0:HEADS]
        block = ctx.enter_context(nc.Block())

        @block.sync
        def _(sp):
            def load_x(i, u):
                sp.dma_start(xin[u], x[bass.ds((i * RING + u) * P, P), :]).then_inc(x_loaded[u], 16)

            def load_strip(u):
                sp.dma_start(wst[:, u, :, :], w_v[:, :, groups[0][1] + u * STRIP:groups[0][1] + (u + 1) * STRIP])\
                    .then_inc(w_loaded[u], 16)

            for u in range(RING):
                load_x(0, u)
            if cum is not None:
                sp.dma_start(wfs, w_v[:, :, 4 * D:4 * D + HEADS]).then_inc(f_in, 16)
                sp.dma_start(bf[:, :], gate_bias.rearrange("(h a) -> h a", a=1)).then_inc(f_in, 16)
            load_strip(0)
            with sp.Fori(1, ST // RING) as i:
                for u in range(RING):
                    sp.wait_ge(x_turned, 2 * RING * i + 2 * u + 2 - 2 * RING)
                    load_x(i, u)
            if cum is not None:
                sp.wait_ge(f_split, 2)
            load_strip(1)
            for g, (kind, col, n, dst) in enumerate(groups):
                nxt = groups[g + 1][1] if g + 1 < len(groups) else None
                assert n % 2 == 0 and n >= 4

                def strip(j, u, load_col):
                    js = first_strip[g] + j
                    if load_col is not None:
                        sp.wait_ge(w_split, js + 1)
                        sp.dma_start(wst[:, u, :, :], w_v[:, :, bass.ds(load_col, STRIP)]).then_inc(w_loaded[u], 16)
                    for q in range(TILES):
                        s = q % RING
                        sp.wait_ge(evac_h, js * TILES + q + 1 + RING)
                        if kind in ("split", "rows"):
                            sp.wait_ge(evac_l, js * TILES + q + 1 + RING)
                        m, c = q // NS, q % NS
                        if kind == "split":
                            sp.dma_start(dst[:, bass.ds(j * STRIP + m * P, P), c * BANK:(c + 1) * BANK]
                                         .rearrange("t p s -> p t s"), raw(stg[:, s, :, :])).then_inc(stored[s], 16)
                        elif kind == "rows":
                            hs = STRIP // HEAD_DIM
                            out = dst[q * 2 * P:(q + 1) * 2 * P, bass.ds(j * hs, hs), :]
                            sp.dma_start(out.rearrange("(t p) h e -> p t (h e)", t=2),
                                         raw(stg[:, s, :, :])).then_inc(stored[s], 16)
                        else:
                            sp.dma_start(dst[bass.ds(j * STRIP + m * P, P), c * BANK:(c + 1) * BANK],
                                         raw(stg[:, s, 0, :])).then_inc(stored[s], 16)

                with sp.Fori(0, n // 2 - 1) as i:
                    for u in range(2):
                        strip(2 * i + u, u, col + (2 * i + u + 2) * STRIP)
                for u in range(2):
                    strip(n - 2 + u, u, None if nxt is None else nxt + u * STRIP)
            if cum is not None:
                sp.wait_ge(f_stored, 64 * NS)
            for s in range(RING):
                sp.wait_ge(stored[s], 16 * total_strips * TILES // RING + 16)

        @block.gpsimd
        def _(pool):
            nc.gpsimd.memset(ident[:, :], 0.0).then_inc(ident_ready, 1)
            pool.wait_ge(ident_ready, 1)
            nc.gpsimd.affine_select(out=ident[:, :], in_=ident[:, :], compare_op=ALU.not_equal, fill=1.0, base=0,
                                    pattern=[[-1, P]], channel_multiplier=1).then_inc(ident_ready, 1)
            if cum is not None:
                nc.gpsimd.memset(raw(wh[:, 1, :, 0:P]), 0.0).then_inc(f_zero, 1)
                nc.gpsimd.memset(raw(wl[:, 1, :, 0:P]), 0.0).then_inc(f_zero, 1)
                for n in range(NS):
                    pool.wait_ge(f_dve, 6 * n + 7)
                    for k in range(4):
                        pool.dma_start(cum[k, :, n * BANK:(n + 1) * BANK], f_out[n][k]).then_inc(f_stored, 16)

        @block.tensor
        def _(pe):
            pe.sem_inc(products, 2 * TILES)
            pe.wait_ge(ident_ready, 2)
            with pe.Fori(0, ST // RING) as i:
                for u in range(RING):
                    pe.wait_ge(x_loaded[u], 16 * i + 16)
                    for b in range(2):
                        k = (2 * u + b) % 4
                        pe.wait_ge(high_out, 2 * RING * i + 2 * u + b + 1)
                        pe.wait_ge(low_out, 2 * RING * i + 2 * u + b + 1)
                        for c in range(4):
                            mm = nc.tensor.transpose(tps[k][:, c, :], xin[u][:, (4 * b + c) * P:(4 * b + c + 1) * P],
                                                     ident[:, :])
                        mm.then_inc(x_turned, 1)
            pe.wait_ge(high_out, 2 * ST + 4)
            pe.wait_ge(low_out, 2 * ST + 4)

            def dot(out, lhs, rhs):
                for c in range(KC):
                    for k, (p, q) in enumerate(((0, 0), (0, 1), (1, 0))):
                        mm = nc.tensor.matmul(out, lhs[p](c), rhs[q](c), start=(c == 0 and k == 0),
                                              stop=(c == KC - 1 and k == 2))
                return mm

            if cum is not None:
                pe.wait_ge(f_split, 2)
                for n in range(NS):
                    dot(tps[n][:, :, :].rearrange("p a b -> p (a b)"),
                        [lambda c, t=t: t[:, 1, c, 0:P] for t in (wh, wl)],
                        [lambda c, t=t: t[:, c, n * BANK:(n + 1) * BANK] for t in (xh, xl)]).then_inc(f_prod, 1)
            for g, (kind, col, n, dst) in enumerate(groups):
                if kind in ("plain", "silu"):
                    pe.wait_ge(evac_l, RING + TILES * sum(m for k, _, m, _ in groups if k in ("split", "rows")))
                with pe.Fori(0, n // 2) as i:
                    for u in range(2):
                        js = first_strip[g] + 2 * i + u
                        pe.wait_ge(w_split, js + 1)
                        for q in range(TILES):
                            pe.wait_ge(evac_h, js * TILES + q + 1)
                            if kind in ("split", "rows"):
                                pe.wait_ge(evac_l, js * TILES + q + 1)
                            m, c0 = q // NS, (q % NS) * BANK
                            if kind == "rows":
                                for b in range(2):
                                    s0 = (2 * q + b) * P
                                    mm = dot(psum[q % RING][:, b * STRIP:(b + 1) * STRIP],
                                             [lambda c, t=t: t[:, c, s0:s0 + P] for t in (xh, xl)],
                                             [lambda c, t=t: t[:, u, c, :] for t in (wh, wl)])
                            else:
                                mm = dot(psum[q % RING][:, :],
                                         [lambda c, t=t: t[:, u, c, m * P:(m + 1) * P] for t in (wh, wl)],
                                         [lambda c, t=t: t[:, c, c0:c0 + BANK] for t in (xh, xl)])
                            mm.then_inc(products, 1)

        def halves(kind, s):
            if kind == "rows":
                v = stg[:, s, :, :].rearrange("p t (h l e) -> p t h l e", l=2, e=HEAD_DIM)
                return v[:, :, :, 0, :], v[:, :, :, 1, :]
            return stg[:, s, 0, :], stg[:, s, 1, :]

        def source(kind, s):
            return psum[s][:, :].rearrange("p (t h e) -> p t h e", t=2, e=HEAD_DIM) if kind == "rows" else psum[s][:, :]

        @block.scalar
        def _(act):
            act.sem_inc(high_out, 4)
            with act.Fori(0, ST // 2) as i:
                for k in range(4):
                    act.wait_ge(x_turned, 4 * i + k + 1)
                    nc.scalar.activation(xh[:, 4 * (k % 2):4 * (k % 2) + 4, bass.ds((2 * i + k // 2) * P, P)],
                                         tps[k][:, :, :], ACT.Copy).then_inc(high_out, 1)
            if cum is not None:
                act.wait_ge(f_in, 32)
                for n in range(NS):
                    act.wait_ge(f_prod, n + 1)
                    nc.scalar.activation(fz[n], tps[n][0:HEADS, :, :].rearrange("p a b -> p (a b)"), ACT.Identity,
                                         bias=bf[:, :]).then_inc(f_act, 1)
                    if n:
                        act.wait_ge(f_scan, n)
                    act.wait_ge(f_act, 4 * n + 1)
                    nc.scalar.activation(fe, fz[n], ACT.Abs).then_inc(f_act, 1)
                    act.wait_ge(f_act, 4 * n + 2)
                    nc.scalar.activation(fe, fe, ACT.Exp, scale=-1.0).then_inc(f_act, 1)
                    act.wait_ge(f_act, 4 * n + 3)
                    nc.scalar.activation(fe, fe, ACT.Ln, bias=1.0).then_inc(f_act, 1)
            act.sem_inc(evac_h, RING)
            for s in range(RING):
                act.sem_inc(stored[s], 16)
            for g, (kind, col, n, dst) in enumerate(groups):
                func = ACT.Silu if kind == "silu" else ACT.Copy
                scale = -HEAD_DIM ** -0.5 if kind == "split" and g == 0 else 1.0
                with act.Fori(0, n // 2) as i:
                    for q in range(2 * TILES):
                        t, s = (first_strip[g] + 2 * i) * TILES + q, q % RING
                        act.wait_ge(products, t + 1 + 2 * TILES)
                        uses = (first_strip[g] + 2 * i) * (TILES // RING) + q // RING
                        act.wait_ge(stored[s], 16 * uses + 16)
                        out = raw(stg[:, s, 0, :]) if kind in ("plain", "silu") else halves(kind, s)[0]
                        nc.scalar.activation(out, source(kind, s), func, scale=scale).then_inc(evac_h, 1)

        @block.vector
        def _(dve):
            dve.sem_inc(low_out, 4)
            dve.sem_inc(evac_l, RING)
            with dve.Fori(0, ST // 2) as i:
                for k in range(4):
                    dve.wait_ge(high_out, 4 * i + k + 1 + 4)
                    at = (slice(None), slice(4 * (k % 2), 4 * (k % 2) + 4), bass.ds((2 * i + k // 2) * P, P))
                    nc.vector.tensor_tensor(xl[at], tps[k][:, :, :], raw(xh[at]), ALU.subtract).then_inc(low_out, 1)
            def split_strip(u, strip, loads):
                dve.wait_ge(w_loaded[u], loads)
                dve.wait_ge(products, (strip + 1) * TILES)
                nc.vector.tensor_copy(wh[:, u, :, :], wst[:, u, :, :]).then_inc(w_high, 1)
                dve.wait_ge(w_high, strip + 1)
                nc.vector.tensor_tensor(wl[:, u, :, :], wst[:, u, :, :], raw(wh[:, u, :, :]), ALU.subtract)\
                    .then_inc(w_split, 1)

            if cum is not None:
                dve.wait_ge(f_in, 32)
                dve.wait_ge(f_zero, 2)
                nc.vector.tensor_copy(wh[:, 1, :, 0:HEADS], wfs).then_inc(f_split, 1)
                dve.wait_ge(f_split, 1)
                nc.vector.tensor_tensor(wl[:, 1, :, 0:HEADS], wfs, raw(wh[:, 1, :, 0:HEADS]), ALU.subtract)\
                    .then_inc(f_split, 1)
            split_strip(0, 0, 16)
            if cum is not None:
                nc.vector.memset(fo, 0.0).then_inc(f_dve, 1)
                for n in range(NS):
                    dve.wait_ge(f_act, 4 * n + 4)
                    nc.vector.scalar_tensor_tensor(out=fe, in0=fz[n], scalar=0.0, in1=fe, op0=ALU.min,
                                                   op1=ALU.subtract).then_inc(f_dve, 1)
                    if n:
                        nc.vector.tensor_copy(last[:, 0:1], fcum[:, BANK - 1:BANK]).then_inc(f_dve, 1)
                    else:
                        nc.vector.memset(last[:, 0:1], 0.0).then_inc(f_dve, 1)
                    dve.wait_ge(f_dve, 6 * n + 3)
                    nc.vector.tensor_tensor_scan(fcum, fe, fo, last[:, 0:1], ALU.add, ALU.add).then_inc(f_scan, 1)
                    dve.wait_ge(f_scan, n + 1)
                    nc.vector.tensor_copy(f_out[n][0].bitcast(F32R), fcum).then_inc(f_dve, 1)
                    nc.vector.tensor_scalar(f_out[n][2].bitcast(F32R), fcum, -1.0, None, ALU.mult).then_inc(f_dve, 1)
                    dve.wait_ge(f_dve, 6 * n + 5)
                    nc.vector.tensor_tensor(f_out[n][1], fcum, f_out[n][0], ALU.subtract).then_inc(f_dve, 1)
                    dve.wait_ge(f_dve, 6 * n + 6)
                    nc.vector.tensor_scalar(f_out[n][3], f_out[n][1], -1.0, None, ALU.mult).then_inc(f_dve, 1)
                dve.wait_ge(f_prod, NS)
            for g, (kind, col, n, dst) in enumerate(groups):
                scale = -HEAD_DIM ** -0.5 if kind == "split" and g == 0 else 1.0
                js = first_strip[g]

                def strip(i, u):
                    split_strip(1 - u, js + 2 * i + u + 1, 8 * (js + 2 * i) + 16 + 16 * u)
                    take_low(i, u)

                def take_low(i, u):
                    if kind not in ("split", "rows"):
                        return
                    for q in range(TILES):
                        s = q % RING
                        dve.wait_ge(evac_h, (js + 2 * i + u) * TILES + q + 1 + RING)
                        hi, lo = halves(kind, s)
                        if scale != 1.0:
                            nc.vector.scalar_tensor_tensor(out=lo, in0=source(kind, s), scalar=scale, in1=raw(hi),
                                                           op0=ALU.mult, op1=ALU.subtract).then_inc(evac_l, 1)
                        else:
                            nc.vector.tensor_tensor(lo, source(kind, s), raw(hi), ALU.subtract).then_inc(evac_l, 1)

                end = n // 2 - (g + 1 == len(groups))
                with dve.Fori(0, end) as i:
                    for u in range(2):
                        strip(i, u)
                if end < n // 2:
                    strip(end, 0)
                    take_low(end, 1)


def wait(engine, sem, value):
    if not isinstance(value, int) or value > 0:
        engine.wait_ge(sem, value)


def alternate(m, n, lag=0):
    return sorted([(0, j) for j in range(m)] + [(1, j) for j in range(n)], key=lambda x: (x[1] + lag * x[0], x[0]))


def attend(nc, stage, qs, ks, vs, gs, cum, ys):
    S = qs.shape[2]
    D = qs.shape[1]
    QT = S // P
    GT = QT // 2
    GW = 2 * P
    STEPS = 2 * QT
    GROUPS = 2 * GT
    PAIRS = D // HEAD_DIM // 2
    PB = BANK // P
    n_chunks = [(s % QT) // PB + 1 for s in range(STEPS)]
    first = [sum(n_chunks[:s]) for s in range(STEPS)]
    CH = sum(n_chunks)
    ROWS = 4
    TURN_LAG = 2
    SB, TB = 2, 4
    assert CH % SB == 0 and CH % TB == 0 and GROUPS % 4 == 0

    def chunks_before(it, s):
        return it * CH + first[s] if s >= 0 else it * CH - CH + first[s + STEPS]

    def width(s, j):
        return min(BANK, (s % QT + 1) * P - j * BANK)

    with ExitStack() as ctx:
        a = Alloc(nc, ctx, stage)
        q1 = [a.sb(f"q1_{i}", [P, S], F32R) for i in range(2)]
        q2 = [a.sb(f"q2_{i}", [P, S], F32R) for i in range(2)]
        k1 = [a.sb(f"k1_{i}", [P, S], F32R) for i in range(2)]
        k2 = [a.sb(f"k2_{i}", [P, S], F32R) for i in range(2)]
        val = [a.sb(f"val{i}", [P, QT, P], F32R) for i in range(2)]
        probs = [a.sb(f"probs{i}", [P, S]) for i in range(ROWS)]
        ph = [a.sb(f"ph{i}", [P, QT, GW], F32R) for i in range(2)]
        pl = [a.sb(f"pl{i}", [P, QT, GW], F32R) for i in range(2)]
        gate = a.sb("gate", [HEAD_DIM, 4, GW])
        low_sum = a.sb("low_sum", [HEAD_DIM, 2, GW])
        scale = a.sb("scale", [HEAD_DIM, 2, GW])
        att = a.sb("att", [HEAD_DIM, 2, GW])
        y = a.sb("y", [HEAD_DIM, GW])
        yh = a.sb("yh", [HEAD_DIM, 2, GW], F32R)
        yl = a.sb("yl", [HEAD_DIM, 2, GW], F32R)
        least = a.sb("least", [P, ROWS, PB])
        den = a.sb("den", [P, 2, 2])
        rden = a.sb("rden", [P, 2, 2])
        ident = a.sb("ident", [P, P])
        identb = a.sb("identb", [P, P], BF16)
        mask = a.sb("mask", [P, P], BF16)
        sps = [a.ps(f"sps{i}", [P, BANK]) for i in range(SB)]
        tps = [a.ps(f"tps{i}", [P, PB, P]) for i in range(TB)]
        ops = [a.ps(f"ops{i}", [P, 2, GW]) for i in range(2)]

        waited = a.sem("waited")
        const_ready = a.sem("const_ready")
        ones_ready = a.sem("ones_ready")
        head_loaded = [a.sem(f"head_loaded{i}") for i in range(2)]
        val_loaded = [a.sem(f"val_loaded{i}") for i in range(2)]
        gate_loaded = [a.sem(f"gate_loaded{i}") for i in range(4)]
        y_stored = [a.sem(f"y_stored{i}") for i in range(2)]
        scored = a.sem("scored")
        scores_out = a.sem("scores_out")
        probs_ready = a.sem("probs_ready")
        turned = a.sem("turned")
        high_out = a.sem("high_out")
        low_out = a.sem("low_out")
        weighed = a.sem("weighed")
        rden_ready = a.sem("rden_ready")
        spread = a.sem("spread")
        moved = a.sem("moved")
        summed = a.sem("summed")
        scaled = a.sem("scaled")
        gated = a.sem("gated")
        y_ready = a.sem("y_ready")
        block = ctx.enter_context(nc.Block())

        @block.sync
        def _(sp):
            def head_rows(h):
                return slice(h * HEAD_DIM, (h + 1) * HEAD_DIM) if isinstance(h, int) else bass.ds(h * HEAD_DIM, HEAD_DIM)

            def load_head(it, hp):
                h = 2 * it + hp
                rows = head_rows(h)
                one = bass.ds(h, 1) if not isinstance(h, int) else slice(h, h + 1)
                wait(sp, scored, chunks_before(it, QT * (hp + 1)) - CH if hp == 0 else it * CH)
                wait(sp, weighed, it * GROUPS - GT if hp == 0 else it * GROUPS)
                sp.sem_inc(waited, 1)
                lo, hi = slice(0, HEAD_DIM), slice(HEAD_DIM, P)
                A = HEAD_DIM
                for n, (dst, src) in enumerate(((q1[hp][lo, :], qs[0, rows, :]), (q1[hp][hi, :], qs[0, rows, :]),
                                 (k1[hp][lo, :], ks[0, rows, :]), (k1[hp][hi, :], ks[1, rows, :]),
                                 (q2[hp][lo, :], qs[1, rows, :]), (k2[hp][lo, :], ks[0, rows, :]),
                                 (q2[hp][A + 2:A + 4, :], cum[2:4, one, :].rearrange("k h s -> (k h) s")),
                                 (k2[hp][A:A + 2, :], cum[0:2, one, :].rearrange("k h s -> (k h) s")))):
                    if n == 6 and isinstance(it, int) and it == 0:
                        sp.wait_ge(ones_ready, 2 * hp + 2)
                    sp.dma_start(raw(dst), src).then_inc(head_loaded[hp], 16)
                sp.dma_start(raw(val[hp][:, :, :]), vs[:, one, :].rearrange("(t p) h e -> p t (h e)", p=P))\
                    .then_inc(val_loaded[hp], 16)

            def load_gate(it, g):
                h = 2 * it + g // GT
                rows = head_rows(h)
                wait(sp, scaled, it * GROUPS + g - 3)
                sp.sem_inc(waited, 1)
                c = g % GT * GW
                sp.dma_start(gate[:, g % 4, :], gs[rows, c:c + GW]).then_inc(gate_loaded[g % 4], 16)

            def pair(it, last):
                for g in range(GROUPS):
                    if not (last and g + 2 >= GROUPS):
                        load_gate(it, g + 2)
                    h = 2 * it + g // GT
                    rows = head_rows(h)
                    wait(sp, y_ready, it * GROUPS + g + 1)
                    sp.sem_inc(waited, 1)
                    c = g % GT * GW
                    sp.dma_start(ys[0, rows, c:c + GW], raw(yh[:, g % 2, :])).then_inc(y_stored[g % 2], 16)
                    sp.dma_start(ys[1, rows, c:c + GW], raw(yl[:, g % 2, :])).then_inc(y_stored[g % 2], 16)
                    if g == 0:
                        load_head(it, 1)
                    if g == GT and not last:
                        load_head(it + 1, 0)

            load_head(0, 0)
            load_gate(0, 0)
            load_gate(0, 1)
            pair(0, False)
            with sp.Fori(1, PAIRS - 1) as it:
                pair(it, False)
            pair(PAIRS - 1, True)
            for i in range(2):
                sp.wait_ge(y_stored[i], 16 * GROUPS * PAIRS)

        @block.gpsimd
        def _(pool):
            for t in (ident, identb, mask):
                nc.gpsimd.memset(t[:, :], 0.0).then_inc(const_ready, 1)
            pool.wait_ge(const_ready, 3)
            for t in (ident, identb):
                nc.gpsimd.affine_select(out=t[:, :], in_=t[:, :], compare_op=ALU.not_equal, fill=1.0, base=0,
                                        pattern=[[-1, P]], channel_multiplier=1).then_inc(const_ready, 1)
            nc.gpsimd.affine_select(out=mask[:, :], in_=mask[:, :], compare_op=ALU.is_ge, fill=MASKED, base=0,
                                    pattern=[[-1, P]], channel_multiplier=1).then_inc(const_ready, 1)

            def pair(it):
                for g in range(GROUPS):
                    n = it * GROUPS + g
                    b = g % 2
                    wait(pool, gate_loaded[g % 4], 16 * (it * (GROUPS // 4) + g // 4 + 1))
                    wait(pool, summed, n + 1)
                    nc.gpsimd.tensor_tensor(scale[:, b, :], scale[:, b, :], gate[:, g % 4, :], ALU.mult)\
                        .then_inc(scaled, 1)
                    wait(pool, y_stored[b], 32 * (it * (GROUPS // 2) + g // 2))
                    wait(pool, scaled, n + 1)
                    wait(pool, y_ready, n)
                    nc.gpsimd.tensor_tensor(yh[:, b, :], att[:, b, :], scale[:, b, :], ALU.mult).then_inc(gated, 1)
                    nc.gpsimd.tensor_tensor(y[:, :], att[:, b, :], scale[:, b, :], ALU.mult).then_inc(gated, 1)
                    wait(pool, gated, 2 * n + 2)
                    nc.gpsimd.tensor_tensor(yl[:, b, :], y[:, :], raw(yh[:, b, :]), ALU.subtract).then_inc(y_ready, 1)

            pair(0)
            with pool.Fori(1, PAIRS) as it:
                pair(it)

        @block.tensor
        def _(pe):
            pe.wait_ge(const_ready, 6)

            def score(it, s, j):
                hp, i = s // QT, s % QT
                if i == 0 and j == 0:
                    wait(pe, head_loaded[hp], 128 * (it + 1))
                c = first[s] + j
                w = width(s, j)
                out = sps[c % SB][:, 0:w]
                wait(pe, scores_out, it * CH + c - SB + 1)
                keys = slice(j * BANK, j * BANK + w)
                last = j == n_chunks[s] - 1
                K = HEAD_DIM + 4
                nc.tensor.matmul(out, q1[hp][:, i * P:(i + 1) * P], k1[hp][:, keys], start=True, stop=False)
                mm = nc.tensor.matmul(out, q2[hp][0:K, i * P:(i + 1) * P], k2[hp][0:K, keys], start=False,
                                      stop=not last)
                if last:
                    mm = nc.tensor.matmul(sps[c % SB][:, w - P:w], identb[:, :], mask[:, :], start=False, stop=True)
                mm.then_inc(scored, 1)

            def turn(it, s, j):
                if j == 0:
                    wait(pe, probs_ready, it * STEPS + s + 1)
                c = first[s] + j
                wait(pe, low_out, it * CH + c - TB + 1)
                for k in range(width(s, j) // P):
                    t0 = (j * PB + k) * P
                    mm = nc.tensor.transpose(tps[c % TB][:, k, :], probs[s % ROWS][:, t0:t0 + P], ident[:, :])
                mm.then_inc(turned, 1)

            def weigh(it, g, lo, hi):
                hp, gh, b = g // GT, g % GT, g % 2
                KT = 2 * gh + 2
                if lo == 0:
                    if gh == 0:
                        wait(pe, val_loaded[hp], 16 * (it + 1))
                    wait(pe, low_out, it * CH + first[2 * g + 1] + n_chunks[2 * g + 1])
                    wait(pe, summed, it * GROUPS + g - 1)
                for kt in range(lo, hi):
                    c0 = P if kt == KT - 1 else 0
                    for t in (ph, pl):
                        mm = nc.tensor.matmul(ops[b][:, 0, c0:GW], val[hp][:, kt, :], t[b][:, kt, c0:GW],
                                              start=(kt == 0 and t is ph), stop=(kt == KT - 1 and t is pl))
                if hi == KT:
                    mm.then_inc(weighed, 1)
                    wait(pe, rden_ready, it * GROUPS + g + 1)
                    for e in range(2):
                        mm = nc.tensor.transpose(ops[b][:, 1, e * P:(e + 1) * P],
                                                 rden[:, b, e:e + 1].to_broadcast([P, P]), ident[:, :])
                    mm.then_inc(spread, 1)

            def step(it, s, begun):
                t_it, t_s = (it, s - TURN_LAG) if s >= TURN_LAG else (it - 1, s - TURN_LAG + STEPS)
                g = (s - TURN_LAG - 2) // 2
                w_it, w_g = (it, g) if g >= 0 else (it - 1, g + GROUPS)
                turning = (s >= TURN_LAG or begun) and t_s < STEPS
                weighing = (g >= 0 or begun) and w_g < GROUPS
                KT = 2 * (w_g % GT) + 2
                lo, hi = (0, KT // 2) if (s - TURN_LAG) % 2 == 0 else (KT // 2, KT)
                scoring = s < STEPS
                scores_now = n_chunks[s] if scoring else 0
                parts = max(scores_now + (n_chunks[t_s] if turning else 0), 1)
                turns = n_chunks[t_s] if turning else 0
                order = alternate(scores_now, turns)
                for j in range(parts):
                    if order and order[j][0]:
                        turn(t_it, t_s, order[j][1])
                    elif order:
                        score(it, s, order[j][1])
                    if weighing:
                        k0, k1_ = (lo + (hi - lo) * (j + d) // parts for d in range(2))
                        if k1_ > k0:
                            weigh(w_it, w_g, k0, k1_)

            for s in range(STEPS):
                step(0, s, False)
            with pe.Fori(1, PAIRS) as it:
                for s in range(STEPS):
                    step(it, s, True)
            for s in range(STEPS, STEPS + 2 + TURN_LAG):
                step(PAIRS - 1, s, True)

        @block.scalar
        def _(act):
            def exps(it, s):
                i, g = s % QT, s // 2
                w = (i + 1) * P
                wait(act, scores_out, it * CH + first[s] + n_chunks[s])
                wait(act, rden_ready, it * GROUPS + g - 1)
                nc.scalar.activation(probs[s % ROWS][:, 0:w], probs[s % ROWS][:, 0:w], ACT.Exp,
                                     bias=least[:, s % ROWS, n_chunks[s] - 1:n_chunks[s]], scale=-1.0,
                                     accum_out=den[:, g % 2, s % 2:s % 2 + 1]).then_inc(probs_ready, 1)

            def high(it, s, j):
                i, g = s % QT, s // 2
                if j == 0:
                    wait(act, weighed, it * GROUPS + g - 1)
                c, n = first[s] + j, width(s, j) // P
                wait(act, turned, it * CH + c + 1)
                nc.scalar.activation(ph[g % 2][:, j * PB:j * PB + n, i % 2 * P:(i % 2 + 1) * P],
                                     tps[c % TB][:, 0:n, :], ACT.Copy).then_inc(high_out, 1)

            def move(it, g):
                b = g % 2
                wait(act, spread, it * GROUPS + g + 1)
                wait(act, y_ready, it * GROUPS + g - 1)
                nc.scalar.activation(low_sum[:, b, :], ops[b][HEAD_DIM:P, 0, :], ACT.Copy).then_inc(moved, 1)
                nc.scalar.activation(scale[:, b, :], ops[b][0:HEAD_DIM, 1, :], ACT.Copy).then_inc(moved, 1)

            def step(it, s, begun):
                def at(d, run):
                    n = s - d
                    if n >= 0 and n < STEPS:
                        run(it, n)
                    elif n < 0 and begun:
                        run(it - 1, n + STEPS)
                at(1, exps)
                at(TURN_LAG, lambda t, n: [high(t, n, j) for j in range(n_chunks[n])])
                if (s - TURN_LAG) % 2 == 0:
                    at(TURN_LAG + 3, lambda t, n: move(t, n // 2))

            for s in range(STEPS):
                step(0, s, False)
            with act.Fori(1, PAIRS) as it:
                for s in range(STEPS):
                    step(it, s, True)
            for s in range(STEPS, STEPS + 3 + TURN_LAG):
                step(PAIRS - 1, s, False)

        @block.vector
        def _(dve):
            for hp in range(2):
                for t in (q2[hp], k2[hp]):
                    nc.vector.memset(raw(t[HEAD_DIM:HEAD_DIM + 4, :]), 1.0).then_inc(ones_ready, 1)

            def take(it, s, j):
                if j == 0:
                    wait(dve, turned, chunks_before(it, s - ROWS + 1))
                c, w = first[s] + j, width(s, j)
                wait(dve, scored, it * CH + c + 1)
                if j:
                    wait(dve, scores_out, it * CH + c)
                nc.vector.tensor_scalar(probs[s % ROWS][:, j * BANK:j * BANK + w], sps[c % SB][:, 0:w], 1.0,
                                        least[:, s % ROWS, j - 1:j] if j else None, ALU.mult, ALU.min,
                                        accum_out=least[:, s % ROWS, j:j + 1]).then_inc(scores_out, 1)

            def low(it, s, j):
                i, g = s % QT, s // 2
                c, n = first[s] + j, width(s, j) // P
                wait(dve, high_out, it * CH + c + 1)
                at = (slice(None), slice(j * PB, j * PB + n), slice(i % 2 * P, (i % 2 + 1) * P))
                nc.vector.tensor_tensor(pl[g % 2][at], tps[c % TB][:, 0:n, :], raw(ph[g % 2][at]), ALU.subtract)\
                    .then_inc(low_out, 1)

            def invert(it, g):
                wait(dve, probs_ready, it * STEPS + 2 * g + 2)
                wait(dve, spread, it * GROUPS + g - 1)
                nc.vector.reciprocal(rden[:, g % 2, :], den[:, g % 2, :]).then_inc(rden_ready, 1)

            def add(it, g):
                b = g % 2
                wait(dve, moved, 2 * (it * GROUPS + g) + 2)
                nc.vector.tensor_tensor(att[:, b, :], ops[b][0:HEAD_DIM, 0, :], low_sum[:, b, :], ALU.add)\
                    .then_inc(summed, 1)

            def step(it, s, begun):
                def at(d, run):
                    n = s - d
                    if n >= 0 and n < STEPS:
                        run(it, n)
                    elif n < 0 and begun:
                        run(it - 1, n + STEPS)
                if s % 2 == 1:
                    at(2, lambda t, n: invert(t, n // 2))
                t_it, t_s = (it, s - TURN_LAG) if s >= TURN_LAG else (it - 1, s - TURN_LAG + STEPS)
                turning = (s >= TURN_LAG or begun) and t_s < STEPS
                scores_now = n_chunks[s] if s < STEPS else 0
                turns = n_chunks[t_s] if turning else 0
                for second, j in alternate(scores_now, turns, 1):
                    if second:
                        low(t_it, t_s, j)
                    else:
                        take(it, s, j)
                if (s - TURN_LAG) % 2 == 0:
                    at(TURN_LAG + 3, lambda t, n: add(t, n // 2))

            for s in range(STEPS):
                step(0, s, False)
            with dve.Fori(1, PAIRS) as it:
                for s in range(STEPS):
                    step(it, s, True)
            for s in range(STEPS, STEPS + 3 + TURN_LAG):
                step(PAIRS - 1, s, False)


def merge(nc, stage, ys, w_out, x, ln_g, ln_b, out):
    S, D = x.shape
    KC, ST = D // P, S // P
    DH = D // BANK
    RING = 4
    YW = 2 * P
    y_v = ys.rearrange("l (c p) s -> p l c s", p=P)
    w_v = w_out.rearrange("(c p) d -> p c d", p=P)
    with ExitStack() as ctx:
        a = Alloc(nc, ctx, stage)
        wst = a.sb("wst", [P, DH, KC, BANK])
        wh = a.sb("wh", [P, KC, D], F32R)
        wl = a.sb("wl", [P, KC, D], F32R)
        yin = [a.sb(f"yin{i}", [P, 2, KC, YW], F32R) for i in range(2)]
        xt = a.sb("xt", [P, RING, D])
        gain = a.sb("gain", [P, D])
        shift = a.sb("shift", [P, D])
        stats = a.sb("stats", [P, 2, DH, 6])
        mean_var = a.sb("mean_var", [P, 2, 2])
        rstd = a.sb("rstd", [P, 2, 2])
        psum = [a.ps(f"ps{i}", [P, DH, BANK]) for i in range(4)]

        w_loaded = [a.sem(f"w_loaded{i}") for i in range(DH)]
        p_loaded = a.sem("p_loaded")
        y_loaded = [a.sem(f"y_loaded{i}") for i in range(2)]
        x_loaded = [a.sem(f"x_loaded{i}") for i in range(RING)]
        stored = [a.sem(f"stored{i}") for i in range(RING)]
        w_split = a.sem("w_split")
        products = a.sem("products")
        summed = a.sem("summed")
        stat = a.sem("stat")
        rooted = a.sem("rooted")
        gathered = a.sem("gathered")
        inverted = a.sem("inverted")
        normed = a.sem("normed")
        gained = a.sem("gained")
        shifted = a.sem("shifted")
        block = ctx.enter_context(nc.Block())

        @block.sync
        def _(sp):
            for h in range(DH):
                sp.dma_start(wst[:, h, :, :], w_v[:, :, h * BANK:(h + 1) * BANK]).then_inc(w_loaded[h], 16)
                if h == 0:
                    for u in range(2):
                        sp.dma_start(raw(yin[u][:, :, :, :]), y_v[:, :, :, u * YW:(u + 1) * YW]).then_inc(y_loaded[u], 16)
            for u in range(RING):
                sp.dma_start(xt[:, u, :], x[u * P:(u + 1) * P, :]).then_inc(x_loaded[u], 16)
            for v, row in ((gain, ln_g), (shift, ln_b)):
                sp.dma_start(v[:, :], row.partition_broadcast(P)).then_inc(p_loaded, 16)

            def tiles(it, last):
                for u in range(RING):
                    n = it * RING + u
                    sp.wait_ge(shifted, n + 1)
                    sp.dma_start(out[bass.ds(n * P, P), :], xt[:, u, :]).then_inc(stored[u], 16)
                    if not last:
                        if u % 2 == 1:
                            b = u // 2
                            sp.dma_start(raw(yin[b][:, :, :, :]), y_v[:, :, :, bass.ds((n + 3) * P, YW)])\
                                .then_inc(y_loaded[b], 16)
                        sp.wait_ge(stored[u], 16 * (it + 1))
                        sp.dma_start(xt[:, u, :], x[bass.ds((n + RING) * P, P), :]).then_inc(x_loaded[u], 16)

            with sp.Fori(0, ST // RING - 1) as it:
                tiles(it, False)
            tiles(ST // RING - 1, True)
            for u in range(RING):
                sp.wait_ge(stored[u], 16 * (ST // RING))

        @block.gpsimd
        def _(pool):
            pool.wait_ge(p_loaded, 32)
            with pool.Fori(0, ST // RING) as it:
                for u in range(RING):
                    n = it * RING + u
                    pool.wait_ge(normed, n + 1)
                    nc.gpsimd.tensor_tensor(xt[:, u, :], xt[:, u, :], gain[:, :], ALU.mult).then_inc(gained, 1)
                    pool.wait_ge(gained, n + 1)
                    nc.gpsimd.tensor_tensor(xt[:, u, :], xt[:, u, :], shift[:, :], ALU.add).then_inc(shifted, 1)

        @block.tensor
        def _(pe):
            def tile(it, u):
                n = it * RING + u
                pe.wait_ge(y_loaded[u // 2], 16 * (it + 1))
                wait(pe, summed, n - 3)
                for h in range(DH):
                    pe.wait_ge(w_split, 2 * h + 2)
                    for c in range(KC):
                        for k, (l, w) in enumerate(((0, wh), (0, wl), (1, wh))):
                            mm = nc.tensor.matmul(psum[u][:, h, :], yin[u // 2][:, l, c, u % 2 * P:(u % 2 + 1) * P],
                                                  w[:, c, h * BANK:(h + 1) * BANK], start=(c == 0 and k == 0),
                                                  stop=(c == KC - 1 and k == 2))
                mm.then_inc(products, 1)

            for u in range(RING):
                tile(0, u)
            with pe.Fori(1, ST // RING) as it:
                for u in range(RING):
                    tile(it, u)

        @block.scalar
        def _(act):
            with act.Fori(0, ST // RING) as it:
                for u in range(RING):
                    act.wait_ge(stat, (it * RING + u + 1) * (DH + 2))
                    nc.scalar.activation(rstd[:, u % 2, 0:1], mean_var[:, u % 2, 1:2], ACT.Sqrt).then_inc(rooted, 1)

        @block.vector
        def _(dve):
            for h in range(DH):
                half = slice(h * BANK, (h + 1) * BANK)
                dve.wait_ge(w_loaded[h], 16)
                nc.vector.tensor_copy(wh[:, :, half], wst[:, h, :, :]).then_inc(w_split, 1)
                dve.wait_ge(w_split, 2 * h + 1)
                nc.vector.tensor_tensor(wl[:, :, half], wst[:, h, :, :], raw(wh[:, :, half]), ALU.subtract)\
                    .then_inc(w_split, 1)

            with dve.Fori(0, ST // RING) as it:
                for u in range(RING):
                    n, b = it * RING + u, u % 2
                    dve.wait_ge(x_loaded[u], 16 * (it + 1))
                    dve.wait_ge(products, n + 1)
                    row = xt[:, u, :].rearrange("p (h d) -> p h d", h=DH)
                    nc.vector.scalar_tensor_tensor(out=row, in0=row, scalar=ALPHA, in1=psum[u][:, :, :],
                                                   op0=ALU.mult, op1=ALU.add).then_inc(summed, 1)
                    dve.wait_ge(summed, n + 1)
                    for h in range(DH):
                        nc.vector.bn_stats(stats[:, b, h, :], row[:, h, :]).then_inc(stat, 1)
                    dve.wait_ge(stat, n * (DH + 2) + DH)
                    dve.sem_inc(gathered, 1)
                    nc.vector.bn_aggr(mean_var[:, b, :], stats[:, b, :, :]).then_inc(stat, 1)
                    dve.wait_ge(stat, n * (DH + 2) + DH + 1)
                    nc.vector.tensor_scalar(mean_var[:, b, 1:2], mean_var[:, b, 1:2], LN_EPS, None, ALU.add)\
                        .then_inc(stat, 1)
                    dve.wait_ge(rooted, n + 1)
                    nc.vector.reciprocal(rstd[:, b, 1:2], rstd[:, b, 0:1]).then_inc(inverted, 1)
                    dve.wait_ge(inverted, n + 1)
                    nc.vector.tensor_scalar(xt[:, u, :], xt[:, u, :], mean_var[:, b, 0:1], rstd[:, b, 1:2],
                                            ALU.subtract, ALU.mult).then_inc(normed, 1)


def recur(nc, stage, us, gs, conv_w, conv_b, w_a, b_a, w_i, b_i, lam, ys):
    D, S = us.shape
    BLOCKS = w_a.shape[0]
    CT = D // BLOCKS // P
    NS = S // BANK
    STEPS = NS
    RING = 4
    HALO = CONV_WIDTH - 1
    STORE_LAG = 4
    KT = D // P
    NPAR = CONV_WIDTH + 4
    u_v = us.rearrange("(t p) s -> p t s", p=P)
    g_v = gs.rearrange("(t p) s -> p t s", p=P)
    y_v = ys.rearrange("l (t p) s -> l p t s", p=P)
    with ExitStack() as ctx:
        a = Alloc(nc, ctx, stage)
        w_st = a.sb("w_st", [P, 2, CT, CT * P])
        w_h = a.sb("w_h", [P, 2, CT, CT * P], F32R)
        w_l = a.sb("w_l", [P, 2, CT, CT * P], F32R)
        rows = a.sb("rows", [NPAR * KT, P])
        par = a.sb("par", [P, NPAR, KT])
        decay = a.sb("decay", [P, KT])
        ndecay = a.sb("ndecay", [P, KT])
        tiny = a.sb("tiny", [P, 8, KT])
        ident = a.sb("ident", [P, P])
        u = [a.sb(f"u{i}", [P, CT, HALO + BANK]) for i in range(RING)]
        uc = [a.sb(f"uc{i}", [P, CT, BANK]) for i in range(RING)]
        uh = [a.sb(f"uh{i}", [P, CT, BANK], F32R) for i in range(2)]
        ul = [a.sb(f"ul{i}", [P, CT, BANK], F32R) for i in range(2)]
        gate = [a.sb(f"gate{i}", [P, CT, BANK]) for i in range(RING)]
        r_ = [a.sb(f"r{i}", [P, CT, BANK]) for i in range(2)]
        a_ = [a.sb(f"a{i}", [P, CT, BANK]) for i in range(2)]
        q_ = [a.sb(f"q{i}", [P, CT, BANK]) for i in range(2)]
        i_ = [a.sb(f"i{i}", [P, CT, BANK]) for i in range(2)]
        h_ = [a.sb(f"h{i}", [P, CT, BANK]) for i in range(2)]
        y = [a.sb(f"y{i}", [P, CT, BANK]) for i in range(2)]
        yh = [a.sb(f"yh{i}", [P, CT, BANK], F32R) for i in range(2)]
        yl = [a.sb(f"yl{i}", [P, CT, BANK], F32R) for i in range(2)]
        zero = a.sb("zero", [P, 1])
        gps = [a.ps(f"gps{i}", [P, 2, CT, BANK]) for i in range(2)]

        w_loaded = a.sem("w_loaded")
        rows_loaded = a.sem("rows_loaded")
        u_loaded = [a.sem(f"u_loaded{i}") for i in range(RING)]
        g_loaded = [a.sem(f"g_loaded{i}") for i in range(RING)]
        stored = [a.sem(f"stored{i}") for i in range(2)]
        const_ready = a.sem("const_ready")
        par_turned = a.sem("par_turned")
        par_ready = a.sem("par_ready")
        par_act = a.sem("par_act")
        decay_ready = a.sem("decay_ready")
        halo_clear = a.sem("halo_clear")
        w_high = a.sem("w_high")
        w_split = a.sem("w_split")
        tapped = a.sem("tapped")
        convolved = a.sem("convolved")
        u_high = a.sem("u_high")
        u_split = a.sem("u_split")
        gates = a.sem("gates")
        waited = a.sem("waited")
        sig = a.sem("sig")
        decayed = a.sem("decayed")
        squared = a.sem("squared")
        inputs = a.sem("inputs")
        rest = a.sem("rest")
        rooted = a.sem("rooted")
        fed = a.sem("fed")
        scanned = a.sem("scanned")
        gated = a.sem("gated")
        y_high = a.sem("y_high")
        y_ready = a.sem("y_ready")
        block = ctx.enter_context(nc.Block())

        def tiles(it, s):
            t0 = it * CT
            sel = slice(t0, t0 + CT) if isinstance(t0, int) else bass.ds(t0, CT)
            return sel, slice(s * BANK, (s + 1) * BANK)

        def column(v, it, s, ct):
            t = it * CT + ct
            return v[:, t:t + 1] if isinstance(t, int) else v[:, bass.ds(t, 1)]

        def each(it, s, begun, d, run):
            n = s - d
            if 0 <= n < STEPS:
                run(it, n)
            elif n < 0 and begun:
                run(it - 1, n + STEPS)

        def all_steps(engine, step, lag):
            for s in range(STEPS):
                step(0, s, False)
            with engine.Fori(1, BLOCKS) as it:
                for s in range(STEPS):
                    step(it, s, True)
            for s in range(STEPS, STEPS + lag):
                step(BLOCKS - 1, s, False)

        @block.sync
        def _(sp):
            def load_w(n):
                for k, w in enumerate((w_a, w_i)):
                    src = w[n:n + 1] if isinstance(n, int) else w[bass.ds(n, 1)]
                    sp.dma_start(w_st[:, k, :, :], src.rearrange("n (c p) d -> p (n c) d", p=P)).then_inc(w_loaded, 16)

            r0 = 0
            for v in (conv_w, conv_b, b_a, b_i, lam):
                src = v.rearrange("k (t p) -> (k t) p", p=P)
                sp.dma_start(rows[r0:r0 + src.shape[0], :], src).then_inc(rows_loaded, 16)
                r0 += src.shape[0]
            load_w(0)
            sp.wait_ge(halo_clear, 2)

            def step(it, s, begun, last=False):
                def load(it, s):
                    b = s % RING
                    sel, pos = tiles(it, s)
                    wait(sp, convolved, (it * STEPS + s - RING + 1) * CT * HALO)
                    if s == 0:
                        sp.dma_start(u[b][:, :, HALO:], u_v[:, sel, pos]).then_inc(u_loaded[b], 16)
                    else:
                        sp.dma_start(u[b][:, :, :], u_v[:, sel, pos.start - HALO:pos.stop]).then_inc(u_loaded[b], 16)
                    wait(sp, gated, it * STEPS + s - RING + 1)
                    sp.dma_start(gate[b][:, :, :], g_v[:, sel, pos]).then_inc(g_loaded[b], 16)
                    if s == 1 and not last:
                        wait(sp, w_split, it + 1)
                        load_w(it + 1)

                def store(it, s):
                    b = s % 2
                    sel, pos = tiles(it, s)
                    wait(sp, y_ready, it * STEPS + s + 1)
                    for l, t in enumerate((yh, yl)):
                        sp.dma_start(y_v[l][:, sel, pos], raw(t[b][:, :, :])).then_inc(stored[b], 16)

                each(it, s, begun, 0, load)
                each(it, s, begun, STORE_LAG, store)

            for s in range(STEPS):
                step(0, s, False)
            with sp.Fori(1, BLOCKS - 1) as it:
                for s in range(STEPS):
                    step(it, s, True)
            for s in range(STEPS + STORE_LAG):
                step(BLOCKS - 1, s, s < STEPS, True)
            for b in range(2):
                sp.wait_ge(stored[b], 16 * STEPS * BLOCKS)

        @block.gpsimd
        def _(pool):
            nc.gpsimd.memset(u[0][:, :, 0:HALO], 0.0).then_inc(halo_clear, 1)
            nc.gpsimd.memset(zero[:, :], 0.0).then_inc(halo_clear, 1)
            nc.gpsimd.memset(ident[:, :], 0.0).then_inc(const_ready, 1)
            pool.wait_ge(const_ready, 1)
            nc.gpsimd.affine_select(out=ident[:, :], in_=ident[:, :], compare_op=ALU.not_equal, fill=1.0, base=0,
                                    pattern=[[-1, P]], channel_multiplier=1).then_inc(const_ready, 1)

            def feed(it, s):
                n = it * STEPS + s
                wait(pool, sig, 4 * n + 4)
                nc.gpsimd.tensor_tensor(i_[s % 2][:, :, :], i_[s % 2][:, :, :], uc[s % RING][:, :, :], ALU.mult)\
                    .then_inc(inputs, 1)

            def gating(it, s):
                b, n = s % 2, it * STEPS + s
                wait(pool, g_loaded[s % RING], 16 * (it * (STEPS // RING) + s // RING + 1))
                wait(pool, scanned, (n + 1) * CT)
                wait(pool, y_ready, n - 1)
                nc.gpsimd.tensor_tensor(y[b][:, :, :], h_[b][:, :, :], gate[s % RING][:, :, :], ALU.mult).then_inc(gated, 1)

            def step(it, s, begun):
                each(it, s, begun, 2, gating)
                each(it, s, begun, 1, feed)

            all_steps(pool, step, 2)

        @block.tensor
        def _(pe):
            pe.wait_ge(rows_loaded, 80)
            pe.wait_ge(const_ready, 2)
            nc.tensor.transpose(gps[0][:, 0, 0, 0:NPAR * KT], rows[:, :], ident[0:NPAR * KT, 0:NPAR * KT])\
                .then_inc(par_turned, 1)
            pe.wait_ge(par_ready, 1)

            def step(it, s, begun):
                b, n = s % 2, it * STEPS + s
                wait(pe, w_split, it + 1)
                wait(pe, u_split, n + 1)
                wait(pe, sig, 4 * (n - 1))
                for k in range(2):
                    for d in range(CT):
                        for c in range(CT):
                            for m, (wt, ut) in enumerate(((w_h, uh), (w_h, ul), (w_l, uh))):
                                mm = nc.tensor.matmul(gps[b][:, k, d, :], wt[:, k, c, d * P:(d + 1) * P],
                                                      ut[b][:, c, :], start=(c == 0 and m == 0),
                                                      stop=(c == CT - 1 and m == 2))
                mm.then_inc(gates, 1)

            all_steps(pe, step, 0)

        TAP, CB, BA, BI, LAM = 0, CONV_WIDTH, CONV_WIDTH + 1, CONV_WIDTH + 2, CONV_WIDTH + 3
        T_ABS, T_EXP, T_ONE, T_LN, T_DIFF, T_SAME, T_REC, T_SP = range(8)

        @block.scalar
        def _(act):
            act.wait_ge(par_ready, 1)
            nc.scalar.activation(tiny[:, T_ABS, :], par[:, LAM, :], ACT.Abs).then_inc(par_act, 1)
            act.wait_ge(par_act, 1)
            nc.scalar.activation(tiny[:, T_EXP, :], tiny[:, T_ABS, :], ACT.Exp, scale=-1.0).then_inc(par_act, 1)
            act.wait_ge(par_ready, 2)
            nc.scalar.activation(tiny[:, T_LN, :], tiny[:, T_ONE, :], ACT.Ln).then_inc(par_act, 1)

            def tap(it, s):
                n, b = it * STEPS + s, s % RING
                wait(act, u_loaded[b], 16 * (it * (STEPS // RING) + s // RING + 1))
                wait(act, inputs, n - 3)
                act.sem_inc(waited, 1)
                for ct in range(CT):
                    nc.scalar.activation(uc[s % RING][:, ct, :], u[b][:, ct, HALO:], ACT.Identity,
                                         bias=column(par[:, CB, :], it, s, ct),
                                         scale=column(par[:, CONV_WIDTH - 1, :], it, s, ct)).then_inc(tapped, 1)

            def nonlinear(it, s):
                n, b = it * STEPS + s, s % 2
                wait(act, decay_ready, 2)
                wait(act, gates, n + 1)
                wait(act, fed, n - 1)
                wait(act, scanned, (n - 1) * CT)
                act.sem_inc(waited, 1)
                for k, (t, bias) in enumerate(((r_, BA), (i_, BI))):
                    for ct in range(CT):
                        nc.scalar.activation(t[b][:, ct, :], gps[b][:, k, ct, :], ACT.Sigmoid,
                                             bias=column(par[:, bias, :], it, s, ct)).then_inc(sig, 1)
                wait(act, sig, 4 * n + 2)
                act.sem_inc(waited, 1)
                for ct in range(CT):
                    nc.scalar.activation(a_[b][:, ct, :], r_[b][:, ct, :], ACT.Exp,
                                         scale=column(ndecay, it, s, ct)).then_inc(decayed, 1)
                wait(act, decayed, 4 * n + 2)
                act.sem_inc(waited, 1)
                for ct in range(CT):
                    nc.scalar.activation(r_[b][:, ct, :], r_[b][:, ct, :], ACT.Tanh,
                                         scale=column(decay, it, s, ct)).then_inc(decayed, 1)
                nc.scalar.activation(q_[b][:, :, :], a_[b][:, :, :], ACT.Square).then_inc(squared, 1)

            def root(it, s):
                n, b = it * STEPS + s, s % 2
                wait(act, rest, n + 1)
                nc.scalar.activation(r_[b][:, :, :], r_[b][:, :, :], ACT.Sqrt).then_inc(rooted, 1)

            def step(it, s, begun):
                each(it, s, begun, 2, root)
                each(it, s, begun, 0, tap)
                each(it, s, begun, 1, nonlinear)

            all_steps(act, step, 2)

        @block.vector
        def _(dve):
            dve.wait_ge(par_turned, 1)
            nc.vector.tensor_copy(par[:, :, :], gps[0][:, 0, 0, 0:NPAR * KT].rearrange("p (k t) -> p k t", k=NPAR))\
                .then_inc(par_ready, 1)
            seq = [0]

            def own(ins):
                seq[0] += 1
                ins.then_inc(w_high, 1)
                dve.wait_ge(w_high, seq[0])

            T = lambda k: tiny[:, k, :]
            dve.wait_ge(par_act, 2)
            nc.vector.tensor_scalar(T(T_ONE), T(T_EXP), 1.0, None, ALU.add).then_inc(par_ready, 1)
            dve.wait_ge(par_ready, 2)
            own(nc.vector.tensor_scalar(T(T_DIFF), T(T_ONE), -1.0, None, ALU.add))
            own(nc.vector.tensor_scalar(T(T_SAME), T(T_DIFF), 0.0, None, ALU.is_equal))
            own(nc.vector.tensor_tensor(T(T_DIFF), T(T_DIFF), T(T_SAME), ALU.add))
            own(nc.vector.reciprocal(T(T_REC), T(T_DIFF)))
            dve.wait_ge(par_act, 3)
            own(nc.vector.tensor_tensor(T(T_SAME), T(T_LN), T(T_SAME), ALU.add))
            own(nc.vector.tensor_tensor(T(T_REC), T(T_REC), T(T_SAME), ALU.mult))
            own(nc.vector.tensor_tensor(T(T_REC), T(T_REC), T(T_EXP), ALU.mult))
            own(nc.vector.tensor_scalar(T(T_SP), par[:, LAM, :], -1.0, 0.0, ALU.mult, ALU.max))
            own(nc.vector.tensor_tensor(T(T_SP), T(T_SP), T(T_REC), ALU.add))
            nc.vector.tensor_scalar(decay[:, :], T(T_SP), LRU_C, None, ALU.mult).then_inc(decay_ready, 1)
            nc.vector.tensor_scalar(ndecay[:, :], T(T_SP), -LRU_C, None, ALU.mult).then_inc(decay_ready, 1)
            OWN = seq[0]

            def split_w(it):
                wait(dve, w_loaded, 32 * (it + 1))
                wait(dve, gates, it * STEPS)
                nc.vector.tensor_copy(w_h[:, :, :, :], w_st[:, :, :, :]).then_inc(w_high, 1)
                wait(dve, w_high, OWN + it + 1)
                nc.vector.tensor_tensor(w_l[:, :, :, :], w_st[:, :, :, :], raw(w_h[:, :, :, :]), ALU.subtract)\
                    .then_inc(w_split, 1)

            def convolve(it, s):
                n, b, ub = it * STEPS + s, s % 2, uc[s % RING]
                for tap in range(HALO):
                    for ct in range(CT):
                        if tap == 0:
                            wait(dve, tapped, n * CT + ct + 1)
                        else:
                            wait(dve, convolved, (n * HALO + tap - 1) * CT + ct + 1)
                        nc.vector.scalar_tensor_tensor(out=ub[:, ct, :], in0=u[s % RING][:, ct, tap:tap + BANK],
                                                       scalar=column(par[:, tap, :], it, s, ct), in1=ub[:, ct, :],
                                                       op0=ALU.mult, op1=ALU.add).then_inc(convolved, 1)
                if s == 0:
                    split_w(it)
                wait(dve, convolved, (n + 1) * HALO * CT)
                wait(dve, gates, n - 1)
                nc.vector.tensor_copy(uh[b][:, :, :], ub[:, :, :]).then_inc(u_high, 1)
                wait(dve, u_high, n + 1)
                nc.vector.tensor_tensor(ul[b][:, :, :], ub[:, :, :], raw(uh[b][:, :, :]), ALU.subtract)\
                    .then_inc(u_split, 1)

            def remainder(it, s):
                n, b = it * STEPS + s, s % 2
                wait(dve, squared, n + 1)
                wait(dve, decayed, 4 * n + 4)
                nc.vector.scalar_tensor_tensor(out=r_[b][:, :, :], in0=q_[b][:, :, :], scalar=1.0, in1=r_[b][:, :, :],
                                               op0=ALU.add, op1=ALU.mult).then_inc(rest, 1)

            def scan(it, s):
                n, b = it * STEPS + s, s % 2
                wait(dve, rooted, n + 1)
                wait(dve, inputs, n + 1)
                nc.vector.tensor_tensor(i_[b][:, :, :], i_[b][:, :, :], r_[b][:, :, :], ALU.mult).then_inc(fed, 1)
                wait(dve, fed, n + 1)
                wait(dve, gated, n - 1)
                for ct in range(CT):
                    start = zero[:, :] if s == 0 else h_[1 - b][:, ct, BANK - 1:BANK]
                    nc.vector.tensor_tensor_scan(h_[b][:, ct, :], a_[b][:, ct, :], i_[b][:, ct, :], start,
                                                 ALU.mult, ALU.add).then_inc(scanned, 1)

            def split_y(it, s):
                n, b = it * STEPS + s, s % 2
                wait(dve, gated, n + 1)
                wait(dve, stored[b], 32 * (it * (STEPS // 2) + s // 2))
                nc.vector.tensor_copy(yh[b][:, :, :], y[b][:, :, :]).then_inc(y_high, 1)
                wait(dve, y_high, n + 1)
                nc.vector.tensor_tensor(yl[b][:, :, :], y[b][:, :, :], raw(yh[b][:, :, :]), ALU.subtract)\
                    .then_inc(y_ready, 1)

            def step(it, s, begun):
                each(it, s, begun, 2, scan)
                each(it, s, begun, 0, convolve)
                each(it, s, begun, 1, remainder)
                each(it, s, begun, 3, split_y)

            all_steps(dve, step, 3)


_INS = ["x", "ln_g", "ln_b", "attn_w_in", "attn_b_f", "attn_w_out", "rnn_w_in", "rnn_conv_w", "rnn_conv_b",
        "rnn_w_a", "rnn_b_a", "rnn_w_i", "rnn_b_i", "rnn_lambda", "rnn_w_out"]


def build(nc, t, out):
    _, S, D = t["x"].shape
    x = t["x"].rearrange("b s d -> (b s) d")
    out = out.rearrange("b s d -> (b s) d")

    def dram(name, shape):
        return nc.dram_tensor(name, shape, F32, kind="Internal").ap()

    qs, ks, ys = (dram(n, (2, D, S)) for n in ("q_halves", "k_halves", "y_halves"))
    vs = dram("v_halves", (S, HEADS, 2 * HEAD_DIM))
    gs, us = dram("gate_path", (D, S)), dram("u_path", (D, S))
    cum = dram("forget_sums", (4, HEADS, S))
    x1 = dram("x1", (S, D))
    n = D // STRIP
    project(nc, "pa", x, t["attn_w_in"][0], [("split", 0, n, qs), ("split", D, n, ks), ("rows", 2 * D, n, vs),
                                              ("silu", 3 * D, n, gs)], t["attn_b_f"][0], cum)
    attend(nc, "at", qs, ks, vs, gs, cum, ys)
    merge(nc, "ma", ys, t["attn_w_out"][0], x, t["ln_g"][0], t["ln_b"][0], x1)
    project(nc, "pr", x1, t["rnn_w_in"][0], [("plain", 0, n, us), ("silu", D, n, gs)])
    recur(nc, "re", us, gs, t["rnn_conv_w"][0], t["rnn_conv_b"], t["rnn_w_a"][0], t["rnn_b_a"], t["rnn_w_i"][0],
          t["rnn_b_i"], t["rnn_lambda"], ys)
    merge(nc, "mr", ys, t["rnn_w_out"][0], x1, t["ln_g"][1], t["ln_b"][1], out)


def kernel(**inputs):
    import numpy as _np
    import concourse.bacc as _bacc
    from concourse import mybir as _mybir
    from concourse.bass_utils import run_bass_kernel_spmd as _run

    nc = _bacc.Bacc("TRN2", target_bir_lowering=False, num_devices=1)
    arrays, args = {}, {}
    for name in _INS:
        v = _np.ascontiguousarray(inputs[name])
        arrays[f"in_{name}"] = v
        args[name] = nc.dram_tensor(f"in_{name}", v.shape, _mybir.dt.from_np(v.dtype), kind="ExternalInput").ap()
    out = nc.dram_tensor("out", inputs["x"].shape, F32, kind="ExternalOutput").ap()
    build(nc, args, out)
    r = _run(nc, [arrays], core_ids=[0])
    return r.results[0]["out"]
```

```python
from contextlib import ExitStack

import concourse.bass as bass
from concourse import mybir

P = 128
BANK = 512
ALU = mybir.AluOpType
ACT = mybir.ActivationFunctionType
F32 = mybir.dt.float32
F32R = mybir.dt.float32r
BF16 = mybir.dt.bfloat16
AX_X = mybir.AxisListType.X

HEADS = 16
HEAD_DIM = 64
CONV_WIDTH = 4
LRU_C = 8.0
LN_EPS = 1e-5
ALPHA = (2.0 * 2) ** 0.25
STRIP = 256
MASKED = 1e30


class Alloc:

    def __init__(self, nc, ctx, stage):
        self.nc, self.ctx, self.stage = nc, ctx, stage

    def sb(self, name, shape, dt=F32):
        return self.ctx.enter_context(self.nc.sbuf_tensor(f"{self.stage}_{name}", shape, dt))

    def ps(self, name, shape, dt=F32):
        return self.ctx.enter_context(self.nc.psum_tensor(f"{self.stage}_{name}", shape, dt))

    def sem(self, name):
        return self.nc.alloc_semaphore(f"{self.stage}_{name}")


def raw(ap):
    return ap.bitcast(F32)


def project(nc, stage, x, w, groups, gate_bias=None, cum=None):
    S, D = x.shape
    KC = D // P
    ST = S // P
    NS = S // BANK
    TILES = 8
    RING = 4
    w_v = w.rearrange("(c p) f -> p c f", p=P)
    with ExitStack() as ctx:
        a = Alloc(nc, ctx, stage)
        xh = a.sb("xh", [P, KC, S], F32R)
        xl = a.sb("xl", [P, KC, S], F32R)
        fbuf = a.sb("fbuf", [P, S])
        fsm = a.sb("fsm", [HEADS, 3, BANK])
        wst = a.sb("wst", [P, 2, KC, STRIP])
        wh = a.sb("wh", [P, 2, KC, STRIP], F32R)
        wl = a.sb("wl", [P, 2, KC, STRIP], F32R)
        stg = a.sb("stg", [P, RING, 2, BANK], F32R)
        ident = a.sb("ident", [P, P])
        bf = a.sb("bf", [HEADS, 1])
        last = a.sb("last", [HEADS, 2])
        warm = a.sb("warm", [P, 1])
        psum = [a.ps(f"ps{i}", [P, BANK]) for i in range(RING)]
        tps = [a.ps(f"tps{i}", [P, 4, P]) for i in range(4)]

        x_loaded = [a.sem(f"x_loaded{i}") for i in range(RING)]
        w_loaded = [a.sem(f"w_loaded{i}") for i in range(2)]
        stored = [a.sem(f"stored{i}") for i in range(RING)]
        ident_ready = a.sem("ident_ready")
        x_turned = a.sem("x_turned")
        high_out = a.sem("high_out")
        low_out = a.sem("low_out")
        w_split = a.sem("w_split")
        w_high = a.sem("w_high")
        products = a.sem("products")
        evac_h = a.sem("evac_h")
        evac_l = a.sem("evac_l")
        if cum is not None:
            f_in, f_zero, f_prod, f_read, f_act, f_dve, f_scan, f_split, f_stored = (
                a.sem(n) for n in ("f_in", "f_zero", "f_prod", "f_read", "f_act", "f_dve", "f_scan", "f_split", "f_stored"))

        total_strips = sum(n for _, _, n, _ in groups)
        first_strip, t = [], 0
        for _, _, n, _ in groups:
            first_strip.append(t)
            t += n
        xin = [raw(stg[:, i, :, :]).rearrange("p a b -> p (a b)") for i in range(RING)]
        fz = [fbuf[0:HEADS, n * BANK:(n + 1) * BANK] for n in range(NS)]
        f_out = [[fbuf[32 * k:32 * k + HEADS, n * BANK:(n + 1) * BANK] for k in range(4)] for n in range(NS)]
        fe, fo, fcum = (fsm[:, k, :] for k in range(3))
        wfs = wst[:, 1, :, 0:HEADS]
        block = ctx.enter_context(nc.Block())

        @block.sync
        def _(sp):
            def load_x(i, u):
                sp.dma_start(xin[u], x[bass.ds((i * RING + u) * P, P), :]).then_inc(x_loaded[u], 16)

            def load_strip(u):
                sp.dma_start(wst[:, u, :, :], w_v[:, :, groups[0][1] + u * STRIP:groups[0][1] + (u + 1) * STRIP])\
                    .then_inc(w_loaded[u], 16)

            load_x(0, 0)
            load_x(0, 1)
            if cum is not None:
                sp.dma_start(wfs, w_v[:, :, 4 * D:4 * D + HEADS]).then_inc(f_in, 16)
                sp.dma_start(bf[:, :], gate_bias.rearrange("(h a) -> h a", a=1)).then_inc(f_in, 16)
            load_x(0, 2)
            load_x(0, 3)
            load_strip(0)
            with sp.Fori(1, ST // RING) as i:
                for u in range(RING):
                    sp.wait_ge(x_turned, 2 * RING * i + 2 * u + 2 - 2 * RING)
                    load_x(i, u)
            if cum is not None:
                sp.wait_ge(f_split, 2)
            load_strip(1)
            for g, (kind, col, n, dst) in enumerate(groups):
                nxt = groups[g + 1][1] if g + 1 < len(groups) else None
                assert n % 2 == 0 and n >= 4

                def strip(j, u, load_col):
                    js = first_strip[g] + j
                    if load_col is not None:
                        sp.wait_ge(w_split, js + 1)
                        sp.dma_start(wst[:, u, :, :], w_v[:, :, bass.ds(load_col, STRIP)]).then_inc(w_loaded[u], 16)
                    for q in range(TILES):
                        s = q % RING
                        sp.wait_ge(evac_h, js * TILES + q + 1 + RING)
                        if kind in ("split", "rows"):
                            sp.wait_ge(evac_l, js * TILES + q + 1 + RING)
                        m, c = q // NS, q % NS
                        if kind == "split":
                            sp.dma_start(dst[:, bass.ds(j * STRIP + m * P, P), c * BANK:(c + 1) * BANK]
                                         .rearrange("t p s -> p t s"), raw(stg[:, s, :, :])).then_inc(stored[s], 16)
                        elif kind == "rows":
                            hs = STRIP // HEAD_DIM
                            out = dst[q * 2 * P:(q + 1) * 2 * P, bass.ds(j * hs, hs), :]
                            sp.dma_start(out.rearrange("(t p) h e -> p t (h e)", t=2),
                                         raw(stg[:, s, :, :])).then_inc(stored[s], 16)
                        else:
                            sp.dma_start(dst[bass.ds(j * STRIP + m * P, P), c * BANK:(c + 1) * BANK],
                                         raw(stg[:, s, 0, :])).then_inc(stored[s], 16)

                with sp.Fori(0, n // 2 - 1) as i:
                    for u in range(2):
                        strip(2 * i + u, u, col + (2 * i + u + 2) * STRIP)
                for u in range(2):
                    strip(n - 2 + u, u, None if nxt is None else nxt + u * STRIP)
            if cum is not None:
                sp.wait_ge(f_stored, 64 * NS)
            for s in range(RING):
                sp.wait_ge(stored[s], 16 * total_strips * TILES // RING + 16)

        @block.gpsimd
        def _(pool):
            nc.gpsimd.memset(ident[:, :], 0.0).then_inc(ident_ready, 1)
            pool.wait_ge(ident_ready, 1)
            nc.gpsimd.affine_select(out=ident[:, :], in_=ident[:, :], compare_op=ALU.not_equal, fill=1.0, base=0,
                                    pattern=[[-1, P]], channel_multiplier=1).then_inc(ident_ready, 1)
            if cum is not None:
                nc.gpsimd.memset(raw(wh[:, 1, :, 0:P]), 0.0).then_inc(f_zero, 1)
                nc.gpsimd.memset(raw(wl[:, 1, :, 0:P]), 0.0).then_inc(f_zero, 1)
                for n in range(NS):
                    pool.wait_ge(f_dve, 6 * n + 7)
                    for k in range(4):
                        pool.dma_start(cum[k, :, n * BANK:(n + 1) * BANK], f_out[n][k]).then_inc(f_stored, 16)

        @block.tensor
        def _(pe):
            pe.sem_inc(products, 2 * TILES)
            pe.wait_ge(ident_ready, 2)

            def turn_chunk(i):
                for u in range(RING):
                    pe.wait_ge(x_loaded[u], 16 * i + 16)
                    for b in range(2):
                        k = (2 * u + b) % 4
                        pe.wait_ge(high_out, 2 * RING * i + 2 * u + b + 1)
                        pe.wait_ge(low_out, 2 * RING * i + 2 * u + b + 1)
                        for c in range(4):
                            mm = nc.tensor.transpose(tps[k][:, c, :], xin[u][:, (4 * b + c) * P:(4 * b + c + 1) * P],
                                                     ident[:, :])
                        mm.then_inc(x_turned, 1)

            def dot(out, lhs, rhs):
                for c in range(KC):
                    for k, (p, q) in enumerate(((0, 0), (0, 1), (1, 0))):
                        mm = nc.tensor.matmul(out, lhs[p](c), rhs[q](c), start=(c == 0 and k == 0),
                                              stop=(c == KC - 1 and k == 2))
                return mm

            def forget_logits(n):
                pe.wait_ge(high_out, 2 * RING * (n + 1) + 4)
                pe.wait_ge(low_out, 2 * RING * (n + 1) + 4)
                if n == 0:
                    pe.wait_ge(f_split, 2)
                dot(psum[n][:, :], [lambda c, t=t: t[:, 1, c, 0:P] for t in (wh, wl)],
                    [lambda c, t=t: t[:, c, n * BANK:(n + 1) * BANK] for t in (xh, xl)]).then_inc(f_prod, 1)

            if cum is not None:
                for n in range(NS):
                    turn_chunk(n)
                    if n:
                        forget_logits(n - 1)
                forget_logits(NS - 1)
            else:
                with pe.Fori(0, NS) as i:
                    turn_chunk(i)
            pe.wait_ge(high_out, 2 * ST + 4)
            pe.wait_ge(low_out, 2 * ST + 4)
            for g, (kind, col, n, dst) in enumerate(groups):
                if kind in ("plain", "silu"):
                    pe.wait_ge(evac_l, RING + TILES * sum(m for k, _, m, _ in groups if k in ("split", "rows")))
                with pe.Fori(0, n // 2) as i:
                    for u in range(2):
                        js = first_strip[g] + 2 * i + u
                        pe.wait_ge(w_split, js + 1)
                        for q in range(TILES):
                            pe.wait_ge(evac_h, js * TILES + q + 1)
                            if kind in ("split", "rows"):
                                pe.wait_ge(evac_l, js * TILES + q + 1)
                            m, c0 = q // NS, (q % NS) * BANK
                            if kind == "rows":
                                for b in range(2):
                                    s0 = (2 * q + b) * P
                                    mm = dot(psum[q % RING][:, b * STRIP:(b + 1) * STRIP],
                                             [lambda c, t=t: t[:, c, s0:s0 + P] for t in (xh, xl)],
                                             [lambda c, t=t: t[:, u, c, :] for t in (wh, wl)])
                            else:
                                mm = dot(psum[q % RING][:, :],
                                         [lambda c, t=t: t[:, u, c, m * P:(m + 1) * P] for t in (wh, wl)],
                                         [lambda c, t=t: t[:, c, c0:c0 + BANK] for t in (xh, xl)])
                            mm.then_inc(products, 1)

        def halves(kind, s):
            if kind == "rows":
                v = stg[:, s, :, :].rearrange("p t (h l e) -> p t h l e", l=2, e=HEAD_DIM)
                return v[:, :, :, 0, :], v[:, :, :, 1, :]
            return stg[:, s, 0, :], stg[:, s, 1, :]

        def source(kind, s):
            return psum[s][:, :].rearrange("p (t h e) -> p t h e", t=2, e=HEAD_DIM) if kind == "rows" else psum[s][:, :]

        @block.scalar
        def _(act):
            act.sem_inc(high_out, 4)
            act.wait_ge(ident_ready, 2)
            nc.scalar.activation(warm[:, :], ident[:, 0:1], ACT.Copy)
            with act.Fori(0, ST // 2) as i:
                for k in range(4):
                    act.wait_ge(x_turned, 4 * i + k + 1)
                    nc.scalar.activation(xh[:, 4 * (k % 2):4 * (k % 2) + 4, bass.ds((2 * i + k // 2) * P, P)],
                                         tps[k][:, :, :], ACT.Copy).then_inc(high_out, 1)
            if cum is not None:
                act.wait_ge(f_in, 32)
                for n in range(NS):
                    act.wait_ge(f_prod, n + 1)
                    nc.scalar.activation(fz[n], psum[n][0:HEADS, :], ACT.Identity, bias=bf[:, :]).then_inc(f_read, 1)
                act.wait_ge(f_read, NS)
            act.sem_inc(evac_h, RING)
            if cum is not None:
                for n in range(NS):
                    if n:
                        act.wait_ge(f_scan, n)
                    nc.scalar.activation(fe, fz[n], ACT.Abs).then_inc(f_act, 1)
                    act.wait_ge(f_act, 3 * n + 1)
                    nc.scalar.activation(fe, fe, ACT.Exp, scale=-1.0).then_inc(f_act, 1)
                    act.wait_ge(f_act, 3 * n + 2)
                    nc.scalar.activation(fe, fe, ACT.Ln, bias=1.0).then_inc(f_act, 1)
            for s in range(RING):
                act.sem_inc(stored[s], 16)
            for g, (kind, col, n, dst) in enumerate(groups):
                func = ACT.Silu if kind == "silu" else ACT.Copy
                scale = -HEAD_DIM ** -0.5 if kind == "split" and g == 0 else 1.0
                with act.Fori(0, n // 2) as i:
                    for q in range(2 * TILES):
                        t, s = (first_strip[g] + 2 * i) * TILES + q, q % RING
                        act.wait_ge(products, t + 1 + 2 * TILES)
                        uses = (first_strip[g] + 2 * i) * (TILES // RING) + q // RING
                        act.wait_ge(stored[s], 16 * uses + 16)
                        out = raw(stg[:, s, 0, :]) if kind in ("plain", "silu") else halves(kind, s)[0]
                        nc.scalar.activation(out, source(kind, s), func, scale=scale).then_inc(evac_h, 1)

        @block.vector
        def _(dve):
            dve.sem_inc(low_out, 4)
            dve.sem_inc(evac_l, RING)
            if cum is not None:
                dve.wait_ge(f_in, 32)
                dve.wait_ge(f_zero, 2)
                nc.vector.tensor_copy(wh[:, 1, :, 0:HEADS], wfs).then_inc(f_split, 1)
                dve.wait_ge(f_split, 1)
                nc.vector.tensor_tensor(wl[:, 1, :, 0:HEADS], wfs, raw(wh[:, 1, :, 0:HEADS]), ALU.subtract)\
                    .then_inc(f_split, 1)
            with dve.Fori(0, ST // 2) as i:
                for k in range(4):
                    dve.wait_ge(high_out, 4 * i + k + 1 + 4)
                    at = (slice(None), slice(4 * (k % 2), 4 * (k % 2) + 4), bass.ds((2 * i + k // 2) * P, P))
                    nc.vector.tensor_tensor(xl[at], tps[k][:, :, :], raw(xh[at]), ALU.subtract).then_inc(low_out, 1)
            def split_strip(u, strip, loads):
                dve.wait_ge(w_loaded[u], loads)
                dve.wait_ge(products, (strip + 1) * TILES)
                nc.vector.tensor_copy(wh[:, u, :, :], wst[:, u, :, :]).then_inc(w_high, 1)
                dve.wait_ge(w_high, strip + 1)
                nc.vector.tensor_tensor(wl[:, u, :, :], wst[:, u, :, :], raw(wh[:, u, :, :]), ALU.subtract)\
                    .then_inc(w_split, 1)

            split_strip(0, 0, 16)
            if cum is not None:
                nc.vector.memset(fo, 0.0).then_inc(f_dve, 1)
                for n in range(NS):
                    dve.wait_ge(f_act, 3 * n + 3)
                    nc.vector.scalar_tensor_tensor(out=fe, in0=fz[n], scalar=0.0, in1=fe, op0=ALU.min,
                                                   op1=ALU.subtract).then_inc(f_dve, 1)
                    if n:
                        nc.vector.tensor_copy(last[:, 0:1], fcum[:, BANK - 1:BANK]).then_inc(f_dve, 1)
                    else:
                        nc.vector.memset(last[:, 0:1], 0.0).then_inc(f_dve, 1)
                    dve.wait_ge(f_dve, 6 * n + 3)
                    nc.vector.tensor_tensor_scan(fcum, fe, fo, last[:, 0:1], ALU.add, ALU.add).then_inc(f_scan, 1)
                    dve.wait_ge(f_scan, n + 1)
                    nc.vector.tensor_copy(f_out[n][0].bitcast(F32R), fcum).then_inc(f_dve, 1)
                    nc.vector.tensor_scalar(f_out[n][2].bitcast(F32R), fcum, -1.0, None, ALU.mult).then_inc(f_dve, 1)
                    dve.wait_ge(f_dve, 6 * n + 5)
                    nc.vector.tensor_tensor(f_out[n][1], fcum, f_out[n][0], ALU.subtract).then_inc(f_dve, 1)
                    dve.wait_ge(f_dve, 6 * n + 6)
                    nc.vector.tensor_scalar(f_out[n][3], f_out[n][1], -1.0, None, ALU.mult).then_inc(f_dve, 1)
                dve.wait_ge(f_prod, NS)
            for g, (kind, col, n, dst) in enumerate(groups):
                scale = -HEAD_DIM ** -0.5 if kind == "split" and g == 0 else 1.0
                js = first_strip[g]

                def strip(i, u):
                    split_strip(1 - u, js + 2 * i + u + 1, 8 * (js + 2 * i) + 16 + 16 * u)
                    take_low(i, u)

                def take_low(i, u):
                    if kind not in ("split", "rows"):
                        return
                    for q in range(TILES):
                        s = q % RING
                        dve.wait_ge(evac_h, (js + 2 * i + u) * TILES + q + 1 + RING)
                        hi, lo = halves(kind, s)
                        if scale != 1.0:
                            nc.vector.scalar_tensor_tensor(out=lo, in0=source(kind, s), scalar=scale, in1=raw(hi),
                                                           op0=ALU.mult, op1=ALU.subtract).then_inc(evac_l, 1)
                        else:
                            nc.vector.tensor_tensor(lo, source(kind, s), raw(hi), ALU.subtract).then_inc(evac_l, 1)

                end = n // 2 - (g + 1 == len(groups))
                with dve.Fori(0, end) as i:
                    for u in range(2):
                        strip(i, u)
                if end < n // 2:
                    strip(end, 0)
                    take_low(end, 1)


def wait(engine, sem, value):
    if not isinstance(value, int) or value > 0:
        engine.wait_ge(sem, value)


def alternate(m, n, lag=0):
    return sorted([(0, j) for j in range(m)] + [(1, j) for j in range(n)], key=lambda x: (x[1] + lag * x[0], x[0]))


def attend(nc, stage, qs, ks, vs, gs, cum, ys):
    S = qs.shape[2]
    D = qs.shape[1]
    QT = S // P
    GT = QT // 2
    GW = 2 * P
    STEPS = 2 * QT
    GROUPS = 2 * GT
    PAIRS = D // HEAD_DIM // 2
    PB = BANK // P
    n_chunks = [(s % QT) // PB + 1 for s in range(STEPS)]
    first = [sum(n_chunks[:s]) for s in range(STEPS)]
    CH = sum(n_chunks)
    ROWS = 4
    TURN_LAG = 3
    SKIP = 3
    SB, TB = 2, 4
    assert CH % SB == 0 and CH % TB == 0 and GROUPS % 4 == 0

    def chunks_before(it, s):
        return it * CH + first[s] if s >= 0 else it * CH - CH + first[s + STEPS]

    def width(s, j):
        return min(BANK, (s % QT + 1) * P - j * BANK)

    with ExitStack() as ctx:
        a = Alloc(nc, ctx, stage)
        q1 = [a.sb(f"q1_{i}", [P, S], F32R) for i in range(2)]
        q2 = [a.sb(f"q2_{i}", [P, S], F32R) for i in range(2)]
        k1 = [a.sb(f"k1_{i}", [P, S], F32R) for i in range(2)]
        k2 = [a.sb(f"k2_{i}", [P, S], F32R) for i in range(2)]
        val = [a.sb(f"val{i}", [P, QT, P], F32R) for i in range(2)]
        probs = [a.sb(f"probs{i}", [P, S]) for i in range(ROWS)]
        ph = [a.sb(f"ph{i}", [P, QT, GW], F32R) for i in range(2)]
        pl = [a.sb(f"pl{i}", [P, QT, GW], F32R) for i in range(2)]
        gate = a.sb("gate", [HEAD_DIM, 4, GW])
        low_sum = a.sb("low_sum", [HEAD_DIM, 2, GW])
        scale = a.sb("scale", [HEAD_DIM, 2, GW])
        att = a.sb("att", [HEAD_DIM, 2, GW])
        y = a.sb("y", [HEAD_DIM, GW])
        yh = a.sb("yh", [HEAD_DIM, 2, GW], F32R)
        yl = a.sb("yl", [HEAD_DIM, 2, GW], F32R)
        least = a.sb("least", [P, ROWS, PB])
        den = a.sb("den", [P, 2, 2])
        rden = a.sb("rden", [P, 2, 2])
        ident = a.sb("ident", [P, P])
        identb = a.sb("identb", [P, P], BF16)
        mask = a.sb("mask", [P, P], BF16)
        sps = [a.ps(f"sps{i}", [P, BANK]) for i in range(SB)]
        tps = [a.ps(f"tps{i}", [P, PB, P]) for i in range(TB)]
        ops = [a.ps(f"ops{i}", [P, 2, GW]) for i in range(2)]

        waited = a.sem("waited")
        const_ready = a.sem("const_ready")
        ones_ready = a.sem("ones_ready")
        head_loaded = [a.sem(f"head_loaded{i}") for i in range(2)]
        val_loaded = [a.sem(f"val_loaded{i}") for i in range(2)]
        gate_loaded = [a.sem(f"gate_loaded{i}") for i in range(4)]
        y_stored = [a.sem(f"y_stored{i}") for i in range(2)]
        scored = a.sem("scored")
        scores_out = a.sem("scores_out")
        probs_ready = a.sem("probs_ready")
        turned = a.sem("turned")
        high_out = a.sem("high_out")
        low_out = a.sem("low_out")
        weighed = a.sem("weighed")
        rden_ready = a.sem("rden_ready")
        spread = a.sem("spread")
        moved = a.sem("moved")
        summed = a.sem("summed")
        scaled = a.sem("scaled")
        gated = a.sem("gated")
        y_ready = a.sem("y_ready")
        block = ctx.enter_context(nc.Block())

        @block.sync
        def _(sp):
            def head_rows(h):
                return slice(h * HEAD_DIM, (h + 1) * HEAD_DIM) if isinstance(h, int) else bass.ds(h * HEAD_DIM, HEAD_DIM)

            def load_head(it, hp):
                h = 2 * it + hp
                rows = head_rows(h)
                one = bass.ds(h, 1) if not isinstance(h, int) else slice(h, h + 1)
                wait(sp, scored, chunks_before(it, QT * (hp + 1)) - CH if hp == 0 else it * CH)
                wait(sp, weighed, it * GROUPS - GT if hp == 0 else it * GROUPS)
                sp.sem_inc(waited, 1)
                lo, hi = slice(0, HEAD_DIM), slice(HEAD_DIM, P)
                A = HEAD_DIM
                for n, (dst, src) in enumerate(((q1[hp][lo, :], qs[0, rows, :]), (q1[hp][hi, :], qs[0, rows, :]),
                                 (k1[hp][lo, :], ks[0, rows, :]), (k1[hp][hi, :], ks[1, rows, :]),
                                 (q2[hp][lo, :], qs[1, rows, :]), (k2[hp][lo, :], ks[0, rows, :]),
                                 (q2[hp][A + 2:A + 4, :], cum[2:4, one, :].rearrange("k h s -> (k h) s")),
                                 (k2[hp][A:A + 2, :], cum[0:2, one, :].rearrange("k h s -> (k h) s")))):
                    if n == 6 and isinstance(it, int) and it == 0:
                        sp.wait_ge(ones_ready, 2 * hp + 2)
                    sp.dma_start(raw(dst), src).then_inc(head_loaded[hp], 16)
                sp.dma_start(raw(val[hp][:, :, :]), vs[:, one, :].rearrange("(t p) h e -> p t (h e)", p=P))\
                    .then_inc(val_loaded[hp], 16)

            def load_gate(it, g):
                h = 2 * it + g // GT
                rows = head_rows(h)
                wait(sp, scaled, it * GROUPS + g - 3)
                sp.sem_inc(waited, 1)
                c = g % GT * GW
                sp.dma_start(gate[:, g % 4, :], gs[rows, c:c + GW]).then_inc(gate_loaded[g % 4], 16)

            def pair(it, last):
                for g in range(GROUPS):
                    if not (last and g + 2 >= GROUPS):
                        load_gate(it, g + 2)
                    h = 2 * it + g // GT
                    rows = head_rows(h)
                    wait(sp, y_ready, it * GROUPS + g + 1)
                    sp.sem_inc(waited, 1)
                    c = g % GT * GW
                    sp.dma_start(ys[0, rows, c:c + GW], raw(yh[:, g % 2, :])).then_inc(y_stored[g % 2], 16)
                    sp.dma_start(ys[1, rows, c:c + GW], raw(yl[:, g % 2, :])).then_inc(y_stored[g % 2], 16)
                    if g == 0:
                        load_head(it, 1)
                    if g == GT and not last:
                        load_head(it + 1, 0)

            load_head(0, 0)
            load_gate(0, 0)
            load_gate(0, 1)
            pair(0, False)
            with sp.Fori(1, PAIRS - 1) as it:
                pair(it, False)
            pair(PAIRS - 1, True)
            for i in range(2):
                sp.wait_ge(y_stored[i], 16 * GROUPS * PAIRS)

        @block.gpsimd
        def _(pool):
            for t in (ident, identb, mask):
                nc.gpsimd.memset(t[:, :], 0.0).then_inc(const_ready, 1)
            pool.wait_ge(const_ready, 3)
            for t in (ident, identb):
                nc.gpsimd.affine_select(out=t[:, :], in_=t[:, :], compare_op=ALU.not_equal, fill=1.0, base=0,
                                        pattern=[[-1, P]], channel_multiplier=1).then_inc(const_ready, 1)
            nc.gpsimd.affine_select(out=mask[:, :], in_=mask[:, :], compare_op=ALU.is_ge, fill=MASKED, base=0,
                                    pattern=[[-1, P]], channel_multiplier=1).then_inc(const_ready, 1)

            def pair(it):
                for g in range(GROUPS):
                    n = it * GROUPS + g
                    b = g % 2
                    wait(pool, gate_loaded[g % 4], 16 * (it * (GROUPS // 4) + g // 4 + 1))
                    wait(pool, moved, 3 * n + 3)
                    nc.gpsimd.tensor_tensor(att[:, b, :], att[:, b, :], low_sum[:, b, :], ALU.add)\
                        .then_inc(summed, 1)
                    nc.gpsimd.tensor_tensor(scale[:, b, :], scale[:, b, :], gate[:, g % 4, :], ALU.mult)\
                        .then_inc(scaled, 1)
                    wait(pool, y_stored[b], 32 * (it * (GROUPS // 2) + g // 2))
                    wait(pool, scaled, n + 1)
                    wait(pool, summed, n + 1)
                    wait(pool, y_ready, n)
                    nc.gpsimd.tensor_tensor(yh[:, b, :], att[:, b, :], scale[:, b, :], ALU.mult).then_inc(gated, 1)
                    nc.gpsimd.tensor_tensor(y[:, :], att[:, b, :], scale[:, b, :], ALU.mult).then_inc(gated, 1)
                    wait(pool, gated, 2 * n + 2)
                    nc.gpsimd.tensor_tensor(yl[:, b, :], y[:, :], raw(yh[:, b, :]), ALU.subtract).then_inc(y_ready, 1)

            pair(0)
            with pool.Fori(1, PAIRS) as it:
                pair(it)

        @block.tensor
        def _(pe):
            pe.wait_ge(const_ready, 6)

            def score(it, s, j):
                hp, i = s // QT, s % QT
                if i == 0 and j == 0:
                    wait(pe, head_loaded[hp], 128 * (it + 1))
                c = first[s] + j
                w = width(s, j)
                out = sps[c % SB][:, 0:w]
                wait(pe, scores_out, it * CH + c - SB + 1)
                keys = slice(j * BANK, j * BANK + w)
                last = j == n_chunks[s] - 1
                K = HEAD_DIM + 4
                nc.tensor.matmul(out, q1[hp][:, i * P:(i + 1) * P], k1[hp][:, keys], start=True, stop=False)
                mm = nc.tensor.matmul(out, q2[hp][0:K, i * P:(i + 1) * P], k2[hp][0:K, keys], start=False,
                                      stop=not last)
                if last:
                    mm = nc.tensor.matmul(sps[c % SB][:, w - P:w], identb[:, :], mask[:, :], start=False, stop=True)
                mm.then_inc(scored, 1)

            def turn(it, s, j):
                if j == 0:
                    wait(pe, probs_ready, it * STEPS + s + 1)
                c = first[s] + j
                wait(pe, low_out, it * CH + c - TB + 1)
                for k in range(width(s, j) // P):
                    t0 = (j * PB + k) * P
                    mm = nc.tensor.transpose(tps[c % TB][:, k, :], probs[s % ROWS][:, t0:t0 + P], ident[:, :])
                mm.then_inc(turned, 1)

            def weigh(it, g, lo, hi):
                hp, gh, b = g // GT, g % GT, g % 2
                KT = 2 * gh + 2
                if lo == 0:
                    if gh == 0:
                        wait(pe, val_loaded[hp], 16 * (it + 1))
                    wait(pe, low_out, it * CH + first[2 * g + 1] + n_chunks[2 * g + 1])
                    wait(pe, moved, 3 * (it * GROUPS + g - 1))
                for kt in range(lo, hi):
                    c0 = P if kt == KT - 1 else 0
                    for t in (ph, pl):
                        mm = nc.tensor.matmul(ops[b][:, 0, c0:GW], val[hp][:, kt, :], t[b][:, kt, c0:GW],
                                              start=(kt == 0 and t is ph), stop=(kt == KT - 1 and t is pl))
                if hi == KT:
                    mm.then_inc(weighed, 1)
                    wait(pe, rden_ready, it * GROUPS + g + 1)
                    for e in range(2):
                        mm = nc.tensor.transpose(ops[b][:, 1, e * P:(e + 1) * P],
                                                 rden[:, b, e:e + 1].to_broadcast([P, P]), ident[:, :])
                    mm.then_inc(spread, 1)

            def step(it, s, begun):
                t_it, t_s = (it, s - TURN_LAG) if s >= TURN_LAG else (it - 1, s - TURN_LAG + STEPS)
                g = (s - TURN_LAG - 2) // 2
                w_it, w_g = (it, g) if g >= 0 else (it - 1, g + GROUPS)
                turning = (s >= TURN_LAG or begun) and t_s < STEPS
                weighing = (g >= 0 or begun) and w_g < GROUPS
                KT = 2 * (w_g % GT) + 2
                lo, hi = (0, KT // 2) if (s - TURN_LAG) % 2 == 0 else (KT // 2, KT)
                scoring = s < STEPS
                scores_now = n_chunks[s] if scoring else 0
                parts = max(scores_now + (n_chunks[t_s] if turning else 0), 1)
                turns = n_chunks[t_s] if turning else 0
                order = alternate(scores_now, turns, -1)
                for j in range(parts):
                    if order and order[j][0]:
                        turn(t_it, t_s, order[j][1])
                    elif order:
                        score(it, s, order[j][1])
                    if weighing:
                        k0, k1_ = (lo + (hi - lo) * max(j + d - SKIP, 0) // max(parts - SKIP, 1) for d in range(2))
                        if j + 1 == parts:
                            k1_ = hi
                        if k1_ > k0:
                            weigh(w_it, w_g, k0, k1_)

            for s in range(STEPS):
                step(0, s, False)
            with pe.Fori(1, PAIRS) as it:
                for s in range(STEPS):
                    step(it, s, True)
            for s in range(STEPS, STEPS + 2 + TURN_LAG):
                step(PAIRS - 1, s, True)

        @block.scalar
        def _(act):
            def exps(it, s):
                i, g = s % QT, s // 2
                w = (i + 1) * P
                wait(act, scores_out, it * CH + first[s] + n_chunks[s])
                wait(act, rden_ready, it * GROUPS + g - 1)
                nc.scalar.activation(probs[s % ROWS][:, 0:w], probs[s % ROWS][:, 0:w], ACT.Exp,
                                     bias=least[:, s % ROWS, n_chunks[s] - 1:n_chunks[s]], scale=-1.0,
                                     accum_out=den[:, g % 2, s % 2:s % 2 + 1]).then_inc(probs_ready, 1)

            def high(it, s, j):
                i, g = s % QT, s // 2
                if j == 0:
                    wait(act, weighed, it * GROUPS + g - 1)
                c, n = first[s] + j, width(s, j) // P
                wait(act, turned, it * CH + c + 1)
                nc.scalar.activation(ph[g % 2][:, j * PB:j * PB + n, i % 2 * P:(i % 2 + 1) * P],
                                     tps[c % TB][:, 0:n, :], ACT.Copy).then_inc(high_out, 1)

            def move(it, g):
                b = g % 2
                wait(act, spread, it * GROUPS + g + 1)
                wait(act, y_ready, it * GROUPS + g - 1)
                nc.scalar.activation(att[:, b, :], ops[b][0:HEAD_DIM, 0, :], ACT.Copy).then_inc(moved, 1)
                nc.scalar.activation(low_sum[:, b, :], ops[b][HEAD_DIM:P, 0, :], ACT.Copy).then_inc(moved, 1)
                nc.scalar.activation(scale[:, b, :], ops[b][0:HEAD_DIM, 1, :], ACT.Copy).then_inc(moved, 1)

            def step(it, s, begun):
                def at(d, run):
                    n = s - d
                    if n >= 0 and n < STEPS:
                        run(it, n)
                    elif n < 0 and begun:
                        run(it - 1, n + STEPS)
                at(TURN_LAG, lambda t, n: [high(t, n, j) for j in range(n_chunks[n])])
                at(1, exps)
                if (s - TURN_LAG) % 2 == 0:
                    at(TURN_LAG + 3, lambda t, n: move(t, n // 2))

            for s in range(STEPS):
                step(0, s, False)
            with act.Fori(1, PAIRS) as it:
                for s in range(STEPS):
                    step(it, s, True)
            for s in range(STEPS, STEPS + 3 + TURN_LAG):
                step(PAIRS - 1, s, False)

        @block.vector
        def _(dve):
            for hp in range(2):
                for t in (q2[hp], k2[hp]):
                    nc.vector.memset(raw(t[HEAD_DIM:HEAD_DIM + 4, :]), 1.0).then_inc(ones_ready, 1)

            def take(it, s, j):
                if j == 0:
                    wait(dve, turned, chunks_before(it, s - ROWS + 1))
                c, w = first[s] + j, width(s, j)
                wait(dve, scored, it * CH + c + 1)
                if j:
                    wait(dve, scores_out, it * CH + c)
                nc.vector.tensor_scalar(probs[s % ROWS][:, j * BANK:j * BANK + w], sps[c % SB][:, 0:w], 1.0,
                                        least[:, s % ROWS, j - 1:j] if j else None, ALU.mult, ALU.min,
                                        accum_out=least[:, s % ROWS, j:j + 1]).then_inc(scores_out, 1)

            def low(it, s, j):
                i, g = s % QT, s // 2
                c, n = first[s] + j, width(s, j) // P
                wait(dve, high_out, it * CH + c + 1)
                at = (slice(None), slice(j * PB, j * PB + n), slice(i % 2 * P, (i % 2 + 1) * P))
                nc.vector.tensor_tensor(pl[g % 2][at], tps[c % TB][:, 0:n, :], raw(ph[g % 2][at]), ALU.subtract)\
                    .then_inc(low_out, 1)

            def invert(it, g):
                wait(dve, probs_ready, it * STEPS + 2 * g + 2)
                wait(dve, spread, it * GROUPS + g - 1)
                nc.vector.reciprocal(rden[:, g % 2, :], den[:, g % 2, :]).then_inc(rden_ready, 1)

            def step(it, s, begun):
                def at(d, run):
                    n = s - d
                    if n >= 0 and n < STEPS:
                        run(it, n)
                    elif n < 0 and begun:
                        run(it - 1, n + STEPS)
                t_it, t_s = (it, s - TURN_LAG) if s >= TURN_LAG else (it - 1, s - TURN_LAG + STEPS)
                turning = (s >= TURN_LAG or begun) and t_s < STEPS
                scores_now = n_chunks[s] if s < STEPS else 0
                turns = n_chunks[t_s] if turning else 0
                for k, (second, j) in enumerate(alternate(scores_now, turns, 1)):
                    if k == 1 and s % 2 == 1:
                        at(2, lambda t, n: invert(t, n // 2))
                    if second:
                        low(t_it, t_s, j)
                    else:
                        take(it, s, j)

            for s in range(STEPS):
                step(0, s, False)
            with dve.Fori(1, PAIRS) as it:
                for s in range(STEPS):
                    step(it, s, True)
            for s in range(STEPS, STEPS + 3 + TURN_LAG):
                step(PAIRS - 1, s, False)


def merge(nc, stage, ys, w_out, x, ln_g, ln_b, out):
    S, D = x.shape
    KC, ST = D // P, S // P
    DH = D // BANK
    RING = 4
    YW = 2 * P
    WP = 4
    CP = KC // WP
    y_v = ys.rearrange("l (c p) s -> p l c s", p=P)
    w_v = w_out.rearrange("(c p) d -> p c d", p=P)
    with ExitStack() as ctx:
        a = Alloc(nc, ctx, stage)
        wst = a.sb("wst", [P, KC, D])
        wh = a.sb("wh", [P, KC, D], F32R)
        wl = a.sb("wl", [P, KC, D], F32R)
        yin = [a.sb(f"yin{i}", [P, 2, KC, YW], F32R) for i in range(2)]
        xt = a.sb("xt", [P, RING, D])
        gain = a.sb("gain", [P, D])
        shift = a.sb("shift", [P, D])
        stats = a.sb("stats", [P, 2, DH, 6])
        mean_var = a.sb("mean_var", [P, 2, 2])
        rstd = a.sb("rstd", [P, 2, 2])
        psum = [a.ps(f"ps{i}", [P, DH, BANK]) for i in range(4)]

        w_loaded = [a.sem(f"w_loaded{i}") for i in range(WP)]
        p_loaded = a.sem("p_loaded")
        y_loaded = [a.sem(f"y_loaded{i}") for i in range(2)]
        x_loaded = [a.sem(f"x_loaded{i}") for i in range(RING)]
        stored = [a.sem(f"stored{i}") for i in range(RING)]
        w_high = a.sem("w_high")
        w_split = a.sem("w_split")
        products = a.sem("products")
        summed = a.sem("summed")
        stat = a.sem("stat")
        rooted = a.sem("rooted")
        gathered = a.sem("gathered")
        inverted = a.sem("inverted")
        normed = a.sem("normed")
        gained = a.sem("gained")
        shifted = a.sem("shifted")
        block = ctx.enter_context(nc.Block())

        @block.sync
        def _(sp):
            for h in range(WP):
                part = slice(h * CP, (h + 1) * CP)
                sp.dma_start(wst[:, part, :], w_v[:, part, :]).then_inc(w_loaded[h], 16)
                if h < 2:
                    sp.dma_start(raw(yin[h][:, :, :, :]), y_v[:, :, :, h * YW:(h + 1) * YW]).then_inc(y_loaded[h], 16)
            for u in range(RING):
                sp.dma_start(xt[:, u, :], x[u * P:(u + 1) * P, :]).then_inc(x_loaded[u], 16)
            for v, row in ((gain, ln_g), (shift, ln_b)):
                sp.dma_start(v[:, :], row.partition_broadcast(P)).then_inc(p_loaded, 16)

            def tiles(it, last):
                for u in range(RING):
                    n = it * RING + u
                    sp.wait_ge(shifted, n + 1)
                    sp.dma_start(out[bass.ds(n * P, P), :], xt[:, u, :]).then_inc(stored[u], 16)
                    if not last:
                        if u % 2 == 1:
                            b = u // 2
                            sp.dma_start(raw(yin[b][:, :, :, :]), y_v[:, :, :, bass.ds((n + 3) * P, YW)])\
                                .then_inc(y_loaded[b], 16)
                        sp.wait_ge(stored[u], 16 * (it + 1))
                        sp.dma_start(xt[:, u, :], x[bass.ds((n + RING) * P, P), :]).then_inc(x_loaded[u], 16)

            with sp.Fori(0, ST // RING - 1) as it:
                tiles(it, False)
            tiles(ST // RING - 1, True)
            for u in range(RING):
                sp.wait_ge(stored[u], 16 * (ST // RING))

        @block.gpsimd
        def _(pool):
            pool.wait_ge(p_loaded, 32)
            with pool.Fori(0, ST // RING) as it:
                for u in range(RING):
                    n = it * RING + u
                    pool.wait_ge(normed, n + 1)
                    nc.gpsimd.tensor_tensor(xt[:, u, :], xt[:, u, :], gain[:, :], ALU.mult).then_inc(gained, 1)
                    pool.wait_ge(gained, n + 1)
                    nc.gpsimd.tensor_tensor(xt[:, u, :], xt[:, u, :], shift[:, :], ALU.add).then_inc(shifted, 1)

        @block.tensor
        def _(pe):
            def tile(it, u):
                n = it * RING + u
                pe.wait_ge(y_loaded[u // 2], 16 * (it + 1))
                wait(pe, summed, n - 3)
                for c in range(KC):
                    if isinstance(it, int) and u == 0 and c % CP == 0:
                        pe.wait_ge(w_split, c // CP + 1)
                    for h in range(DH):
                        for k, (l, w) in enumerate(((0, wh), (0, wl), (1, wh))):
                            mm = nc.tensor.matmul(psum[u][:, h, :], yin[u // 2][:, l, c, u % 2 * P:(u % 2 + 1) * P],
                                                  w[:, c, h * BANK:(h + 1) * BANK], start=(c == 0 and k == 0),
                                                  stop=(c == KC - 1 and k == 2))
                mm.then_inc(products, 1)

            for u in range(RING):
                tile(0, u)
            with pe.Fori(1, ST // RING) as it:
                for u in range(RING):
                    tile(it, u)

        @block.scalar
        def _(act):
            for h in range(WP):
                part = slice(h * CP, (h + 1) * CP)
                act.wait_ge(w_loaded[h], 16)
                nc.scalar.activation(wh[:, part, :], wst[:, part, :], ACT.Copy).then_inc(w_high, 1)

            with act.Fori(0, ST // RING) as it:
                for u in range(RING):
                    act.wait_ge(stat, (it * RING + u + 1) * (DH + 2))
                    nc.scalar.activation(rstd[:, u % 2, 0:1], mean_var[:, u % 2, 1:2], ACT.Sqrt).then_inc(rooted, 1)

        @block.vector
        def _(dve):
            for h in range(WP):
                part = slice(h * CP, (h + 1) * CP)
                dve.wait_ge(w_high, h + 1)
                nc.vector.tensor_tensor(wl[:, part, :], wst[:, part, :], raw(wh[:, part, :]), ALU.subtract)\
                    .then_inc(w_split, 1)

            with dve.Fori(0, ST // RING) as it:
                for u in range(RING):
                    n, b = it * RING + u, u % 2
                    dve.wait_ge(x_loaded[u], 16 * (it + 1))
                    dve.wait_ge(products, n + 1)
                    row = xt[:, u, :].rearrange("p (h d) -> p h d", h=DH)
                    nc.vector.scalar_tensor_tensor(out=row, in0=row, scalar=ALPHA, in1=psum[u][:, :, :],
                                                   op0=ALU.mult, op1=ALU.add).then_inc(summed, 1)
                    dve.wait_ge(summed, n + 1)
                    for h in range(DH):
                        nc.vector.bn_stats(stats[:, b, h, :], row[:, h, :]).then_inc(stat, 1)
                    dve.wait_ge(stat, n * (DH + 2) + DH)
                    dve.sem_inc(gathered, 1)
                    nc.vector.bn_aggr(mean_var[:, b, :], stats[:, b, :, :]).then_inc(stat, 1)
                    dve.wait_ge(stat, n * (DH + 2) + DH + 1)
                    nc.vector.tensor_scalar(mean_var[:, b, 1:2], mean_var[:, b, 1:2], LN_EPS, None, ALU.add)\
                        .then_inc(stat, 1)
                    dve.wait_ge(rooted, n + 1)
                    nc.vector.reciprocal(rstd[:, b, 1:2], rstd[:, b, 0:1]).then_inc(inverted, 1)
                    dve.wait_ge(inverted, n + 1)
                    nc.vector.tensor_scalar(xt[:, u, :], xt[:, u, :], mean_var[:, b, 0:1], rstd[:, b, 1:2],
                                            ALU.subtract, ALU.mult).then_inc(normed, 1)


def recur(nc, stage, us, gs, conv_w, conv_b, w_a, b_a, w_i, b_i, lam, w_out, x, ln_g, ln_b, out):
    D, S = us.shape
    BLOCKS = w_a.shape[0]
    CT = D // BLOCKS // P
    KT = D // P
    W = 2 * P
    FT = KT // 2
    NB = BLOCKS // 2
    STEPS = 4
    TURNS = S // W * 2 // STEPS
    DH = D // BANK
    SLOTS = 4
    PIECES = BLOCKS + KT
    HALO = CONV_WIDTH - 1
    NPAR = CONV_WIDTH + 4
    u_v = us.rearrange("(t p) s -> p t s", p=P)
    g_v = gs.rearrange("(t p) s -> p t s", p=P)
    o_v = w_out.rearrange("(c p) d -> p c d", p=P)
    with ExitStack() as ctx:
        a = Alloc(nc, ctx, stage)
        w_h = a.sb("w_h", [P, BLOCKS, 2, CT, CT * P], F32R)
        w_l = a.sb("w_l", [P, BLOCKS, 2, CT, CT * P], F32R)
        o_h = a.sb("o_h", [P, KT, D], F32R)
        o_l = a.sb("o_l", [P, KT, D], F32R)
        xt = a.sb("xt", [P, SLOTS, D])
        gain = a.sb("gain", [P, D])
        shift = a.sb("shift", [P, D])
        stats = a.sb("stats", [P, 2, DH, 6])
        mean_var = a.sb("mean_var", [P, 2, 2])
        rstd = a.sb("rstd", [P, 2, 2])
        rows = a.sb("rows", [NPAR * KT, P])
        par = a.sb("par", [P, NPAR, KT])
        decay = a.sb("decay", [P, KT])
        ndecay = a.sb("ndecay", [P, KT])
        tiny = a.sb("tiny", [P, 8, KT])
        ident = a.sb("ident", [P, P])
        u = [a.sb(f"u{i}", [P, FT, HALO + W]) for i in range(2)]
        uc = [a.sb(f"uc{i}", [P, FT, W]) for i in range(2)]
        uh = a.sb("uh", [P, FT, W], F32R)
        ul = a.sb("ul", [P, FT, W], F32R)
        gate = [a.sb(f"gate{i}", [P, FT, W]) for i in range(2)]
        r_ = [a.sb(f"r{i}", [P, FT, W]) for i in range(2)]
        a_ = [a.sb(f"a{i}", [P, FT, W]) for i in range(2)]
        q_ = a.sb("q", [P, FT, W])
        i_ = [a.sb(f"i{i}", [P, FT, W]) for i in range(2)]
        h_ = [a.sb(f"h{i}", [P, FT, W]) for i in range(2)]
        yh = a.sb("yh", [P, FT, W], F32R)
        yl = a.sb("yl", [P, FT, W], F32R)
        gps = a.ps("gps", [P, 2, FT, W])
        ops = [a.ps(f"ops{i}", [P, DH, BANK]) for i in range(2)]

        w_loaded = [a.sem(f"w_loaded{i}") for i in range(SLOTS)]
        w_split = a.sem("w_split")
        rows_loaded = a.sem("rows_loaded")
        p_loaded = a.sem("p_loaded")
        u_loaded = [a.sem(f"u_loaded{i}") for i in range(2)]
        g_loaded = [a.sem(f"g_loaded{i}") for i in range(2)]
        x_loaded = [a.sem(f"x_loaded{i}") for i in range(SLOTS)]
        stored = [a.sem(f"stored{i}") for i in range(SLOTS)]
        waited = a.sem("waited")
        const_ready = a.sem("const_ready")
        par_turned = a.sem("par_turned")
        par_ready = a.sem("par_ready")
        par_act = a.sem("par_act")
        par_own = a.sem("par_own")
        decay_ready = a.sem("decay_ready")
        clear = a.sem("clear")
        tapped = a.sem("tapped")
        convolved = a.sem("convolved")
        u_split = a.sem("u_split")
        gates = a.sem("gates")
        sig = a.sem("sig")
        decayed = a.sem("decayed")
        squared = a.sem("squared")
        inputs = a.sem("inputs")
        rest = a.sem("rest")
        rooted = a.sem("rooted")
        fed = a.sem("fed")
        scanned = a.sem("scanned")
        gated = a.sem("gated")
        y_split = a.sem("y_split")
        merged = a.sem("merged")
        summed = a.sem("summed")
        stat = a.sem("stat")
        gathered = a.sem("gathered")
        dev_ready = a.sem("dev_ready")
        inverted = a.sem("inverted")
        normed = a.sem("normed")
        scaled = a.sem("scaled")
        block = ctx.enter_context(nc.Block())

        def each(it, s, begun, d, run):
            n = s - d
            if 0 <= n < STEPS:
                run(it, n)
            elif n < 0 and begun:
                run(it - 1, n + STEPS)

        def all_steps(engine, step):
            for s in range(STEPS):
                step(0, s, False)
            with engine.Fori(1, TURNS) as it:
                for s in range(STEPS):
                    step(it, s, True)
            for s in range(STEPS, 2 * STEPS):
                step(TURNS - 1, s, False)

        def slots(s):
            return range(s // 2 * 2, s // 2 * 2 + 2)

        def features(s):
            return slice(s % 2 * FT, (s % 2 + 1) * FT)

        def column(v, s, t):
            k = s % 2 * FT + t
            return v[:, k:k + 1]

        @block.sync
        def _(sp):
            r0 = 0
            for v in (conv_w, conv_b, b_a, b_i, lam):
                src = v.rearrange("k (t p) -> (k t) p", p=P)
                sp.dma_start(rows[r0:r0 + src.shape[0], :], src).then_inc(rows_loaded, 16)
                r0 += src.shape[0]

            def load_piece(k):
                slot = k % SLOTS
                wait(sp, w_split, 2 * (k - SLOTS) + 2)
                if k < BLOCKS:
                    for g, w in enumerate((w_a, w_i)):
                        dst = xt[:, slot, g * CT * CT * P:(g + 1) * CT * CT * P].rearrange("p (c d) -> p c d", c=CT)
                        sp.dma_start(dst, w[k].rearrange("(c p) d -> p c d", p=P)).then_inc(w_loaded[slot], 16)
                else:
                    sp.dma_start(xt[:, slot, :], o_v[:, k - BLOCKS, :]).then_inc(w_loaded[slot], 16)

            def load_u(it, s):
                b = s % 2
                wait(sp, convolved, (it * STEPS + s - 1) * FT * HALO)
                sp.sem_inc(waited, 1)
                if isinstance(it, int) and it == 0 and s < 2:
                    sp.dma_start(u[b][:, :, HALO:], u_v[:, features(s), 0:W]).then_inc(u_loaded[b], 16)
                else:
                    pos = bass.ds((2 * it + s // 2) * W - HALO, HALO + W)
                    sp.dma_start(u[b][:, :, :], u_v[:, features(s), pos]).then_inc(u_loaded[b], 16)

            def load_gate(it, s):
                b = s % 2
                wait(sp, y_split, 2 * (it * STEPS + s - 1))
                sp.sem_inc(waited, 1)
                sp.dma_start(gate[b][:, :, :], g_v[:, features(s), bass.ds((2 * it + s // 2) * W, W)])\
                    .then_inc(g_loaded[b], 16)

            def load_x(it, s):
                if s % 2 == 0:
                    return
                wait(sp, w_split, 2 * PIECES)
                for k in slots(s):
                    wait(sp, stored[k], 16 * it + 16)
                sp.sem_inc(waited, 1)
                for k in slots(s):
                    sp.dma_start(xt[:, k, :], x[bass.ds((SLOTS * it + k) * P, P), :]).then_inc(x_loaded[k], 16)

            def store(it, s):
                if s % 2 == 0:
                    return
                for k in slots(s):
                    n = it * SLOTS + k
                    wait(sp, scaled, 2 * n + 2)
                    sp.sem_inc(waited, 1)
                    sp.dma_start(out[bass.ds(n * P, P), :], xt[:, k, :]).then_inc(stored[k], 16)

            def step(it, s, begun, last=False):
                if s + 1 < STEPS:
                    load_u(it, s + 1)
                elif not last:
                    load_u(it + 1, 0)
                each(it, s, begun, 1, load_gate)
                each(it, s, begun, 3, load_x)
                each(it, s, begun, 4, store)

            for k in range(SLOTS):
                sp.sem_inc(stored[k], 16)
            load_u(0, 0)
            for k in range(BLOCKS):
                load_piece(k)
            load_u(0, 1)
            for k in range(BLOCKS, PIECES):
                load_piece(k)
            for v, row in ((gain, ln_g), (shift, ln_b)):
                sp.dma_start(v[:, :], row.partition_broadcast(P)).then_inc(p_loaded, 16)
            for s in range(1, STEPS):
                step(0, s, False)
            with sp.Fori(1, TURNS - 1) as it:
                for s in range(STEPS):
                    step(it, s, True)
            for s in range(STEPS):
                step(TURNS - 1, s, True, True)
            for s in range(STEPS, 2 * STEPS):
                each(TURNS - 1, s, False, 1, load_gate)
                each(TURNS - 1, s, False, 3, load_x)
                each(TURNS - 1, s, False, 4, store)
            for k in range(SLOTS):
                sp.wait_ge(stored[k], 16 * TURNS + 16)

        @block.gpsimd
        def _(pool):
            for b in range(2):
                nc.gpsimd.memset(u[b][:, :, 0:HALO], 0.0).then_inc(clear, 1)
                nc.gpsimd.memset(h_[b][:, :, W - 1:W], 0.0).then_inc(clear, 1)
            nc.gpsimd.memset(ident[:, :], 0.0).then_inc(const_ready, 1)
            pool.wait_ge(const_ready, 1)
            nc.gpsimd.affine_select(out=ident[:, :], in_=ident[:, :], compare_op=ALU.not_equal, fill=1.0, base=0,
                                    pattern=[[-1, P]], channel_multiplier=1).then_inc(const_ready, 1)

            def feed(it, s):
                b, n = s % 2, it * STEPS + s
                wait(pool, sig, 2 * FT * (n + 1))
                nc.gpsimd.tensor_tensor(i_[b][:, :, :], i_[b][:, :, :], uc[b][:, :, :], ALU.mult).then_inc(inputs, 1)

            def gating(it, s):
                b, n = s % 2, it * STEPS + s
                wait(pool, g_loaded[b], 16 * (it * (STEPS // 2) + s // 2 + 1))
                wait(pool, scanned, (n + 1) * FT)
                nc.gpsimd.tensor_tensor(gate[b][:, :, :], h_[b][:, :, :], gate[b][:, :, :], ALU.mult).then_inc(gated, 1)

            def finish(it, s):
                if s % 2 == 0:
                    return
                if isinstance(it, int) and it == 0:
                    wait(pool, p_loaded, 32)
                for k in slots(s):
                    n = it * SLOTS + k
                    wait(pool, normed, n + 1)
                    nc.gpsimd.tensor_tensor(xt[:, k, :], xt[:, k, :], gain[:, :], ALU.mult).then_inc(scaled, 1)
                    wait(pool, scaled, 2 * n + 1)
                    nc.gpsimd.tensor_tensor(xt[:, k, :], xt[:, k, :], shift[:, :], ALU.add).then_inc(scaled, 1)

            def step(it, s, begun):
                each(it, s, begun, 1, feed)
                each(it, s, begun, 2, gating)
                each(it, s, begun, 4, finish)

            all_steps(pool, step)

        @block.tensor
        def _(pe):
            pe.wait_ge(rows_loaded, 80)
            pe.wait_ge(const_ready, 2)
            nc.tensor.transpose(gps[:, 0, 0, 0:NPAR * KT], rows[:, :], ident[0:NPAR * KT, 0:NPAR * KT])\
                .then_inc(par_turned, 1)
            pe.wait_ge(par_ready, 1)

            def gate_products(it, s):
                n = it * STEPS + s
                if isinstance(it, int) and it == 0:
                    wait(pe, w_split, 2 * NB * (s % 2 + 1))
                wait(pe, u_split, 2 * n + 2)
                wait(pe, sig, 2 * FT * n)
                for k in range(2):
                    for t in range(FT):
                        j, d = s % 2 * NB + t // CT, t % CT
                        for c in range(CT):
                            for m, (wt, ut) in enumerate(((w_h, uh), (w_h, ul), (w_l, uh))):
                                mm = nc.tensor.matmul(gps[:, k, t, :], wt[:, j, k, c, d * P:(d + 1) * P],
                                                      ut[:, t // CT * CT + c, :], start=(c == 0 and m == 0),
                                                      stop=(c == CT - 1 and m == 2))
                mm.then_inc(gates, 1)

            def merge_products(it, s):
                n, hf = it * STEPS + s, s % 2
                wait(pe, y_split, 2 * n + 2)
                if hf == 0:
                    wait(pe, summed, n)
                if isinstance(it, int) and it == 0:
                    wait(pe, w_split, 2 * BLOCKS + 2 * FT * (hf + 1))
                for t in range(2):
                    for h in range(DH):
                        for c in range(FT):
                            for m, (yt, wt) in enumerate(((yh, o_h), (yh, o_l), (yl, o_h))):
                                mm = nc.tensor.matmul(ops[t][:, h, :], yt[:, c, t * P:(t + 1) * P],
                                                      wt[:, hf * FT + c, h * BANK:(h + 1) * BANK],
                                                      start=(hf == 0 and c == 0 and m == 0),
                                                      stop=(hf == 1 and c == FT - 1 and m == 2))
                mm.then_inc(merged, 1)

            def step(it, s, begun):
                each(it, s, begun, 0, gate_products)
                each(it, s, begun, 3, merge_products)

            all_steps(pe, step)

        TAP, CB, BA, BI, LAM = 0, CONV_WIDTH, CONV_WIDTH + 1, CONV_WIDTH + 2, CONV_WIDTH + 3
        T_ABS, T_EXP, T_ONE, T_LN, T_DIFF, T_SAME, T_REC, T_SP = range(8)

        @block.scalar
        def _(act):
            act.wait_ge(par_ready, 1)
            nc.scalar.activation(tiny[:, T_ABS, :], par[:, LAM, :], ACT.Abs).then_inc(par_act, 1)
            act.wait_ge(par_act, 1)
            nc.scalar.activation(tiny[:, T_EXP, :], tiny[:, T_ABS, :], ACT.Exp, scale=-1.0).then_inc(par_act, 1)
            act.wait_ge(par_ready, 2)
            nc.scalar.activation(tiny[:, T_LN, :], tiny[:, T_ONE, :], ACT.Ln).then_inc(par_act, 1)

            def tap(it, s):
                n, b = it * STEPS + s, s % 2
                wait(act, u_loaded[b], 16 * (it * (STEPS // 2) + s // 2 + 1))
                wait(act, inputs, n - 1)
                for t in range(FT):
                    nc.scalar.activation(uc[b][:, t, :], u[b][:, t, HALO:], ACT.Identity,
                                         bias=column(par[:, CB, :], s, t),
                                         scale=column(par[:, CONV_WIDTH - 1, :], s, t)).then_inc(tapped, 1)

            def nonlinear(it, s):
                n, b = it * STEPS + s, s % 2
                if isinstance(it, int) and n == 0:
                    act.wait_ge(decay_ready, 2)
                wait(act, gates, n + 1)
                wait(act, scanned, (n - 1) * FT)
                for k, (v, bias) in enumerate(((r_, BA), (i_, BI))):
                    for t in range(FT):
                        nc.scalar.activation(v[b][:, t, :], gps[:, k, t, :], ACT.Sigmoid,
                                             bias=column(par[:, bias, :], s, t)).then_inc(sig, 1)
                wait(act, sig, 2 * FT * n + FT)
                for t in range(FT):
                    nc.scalar.activation(a_[b][:, t, :], r_[b][:, t, :], ACT.Exp,
                                         scale=column(ndecay, s, t)).then_inc(decayed, 1)
                wait(act, decayed, 2 * FT * n + FT)
                for t in range(FT):
                    nc.scalar.activation(r_[b][:, t, :], r_[b][:, t, :], ACT.Tanh,
                                         scale=column(decay, s, t)).then_inc(decayed, 1)
                wait(act, rest, n)
                nc.scalar.activation(q_[:, :, :], a_[b][:, :, :], ACT.Square).then_inc(squared, 1)

            def root(it, s):
                n, b = it * STEPS + s, s % 2
                wait(act, rest, n + 1)
                nc.scalar.activation(r_[b][:, :, :], r_[b][:, :, :], ACT.Sqrt).then_inc(rooted, 1)

            def deviation(it, s):
                if s % 2 == 1:
                    for k in slots(s):
                        act.wait_ge(stat, (it * SLOTS + k + 1) * (DH + 2))
                        nc.scalar.activation(rstd[:, k % 2, 0:1], mean_var[:, k % 2, 1:2], ACT.Sqrt)\
                            .then_inc(dev_ready, 1)

            def step(it, s, begun):
                each(it, s, begun, 0, tap)
                each(it, s, begun, 2, root)
                each(it, s, begun, 1, nonlinear)
                each(it, s, begun, 4, deviation)

            all_steps(act, step)

        @block.vector
        def _(dve):
            dve.wait_ge(par_turned, 1)
            nc.vector.tensor_copy(par[:, :, :], gps[:, 0, 0, 0:NPAR * KT].rearrange("p (k t) -> p k t", k=NPAR))\
                .then_inc(par_ready, 1)
            seq = [0]

            def own(ins):
                seq[0] += 1
                ins.then_inc(par_own, 1)
                dve.wait_ge(par_own, seq[0])

            T = lambda k: tiny[:, k, :]
            dve.wait_ge(par_act, 2)
            nc.vector.tensor_scalar(T(T_ONE), T(T_EXP), 1.0, None, ALU.add).then_inc(par_ready, 1)
            dve.wait_ge(par_ready, 2)
            own(nc.vector.tensor_scalar(T(T_DIFF), T(T_ONE), -1.0, None, ALU.add))
            own(nc.vector.tensor_scalar(T(T_SAME), T(T_DIFF), 0.0, None, ALU.is_equal))
            own(nc.vector.tensor_tensor(T(T_DIFF), T(T_DIFF), T(T_SAME), ALU.add))
            own(nc.vector.reciprocal(T(T_REC), T(T_DIFF)))
            dve.wait_ge(par_act, 3)
            own(nc.vector.tensor_tensor(T(T_SAME), T(T_LN), T(T_SAME), ALU.add))
            own(nc.vector.tensor_tensor(T(T_REC), T(T_REC), T(T_SAME), ALU.mult))
            own(nc.vector.tensor_tensor(T(T_REC), T(T_REC), T(T_EXP), ALU.mult))
            own(nc.vector.tensor_scalar(T(T_SP), par[:, LAM, :], -1.0, 0.0, ALU.mult, ALU.max))
            own(nc.vector.tensor_tensor(T(T_SP), T(T_SP), T(T_REC), ALU.add))
            nc.vector.tensor_scalar(decay[:, :], T(T_SP), LRU_C, None, ALU.mult).then_inc(decay_ready, 1)
            nc.vector.tensor_scalar(ndecay[:, :], T(T_SP), -LRU_C, None, ALU.mult).then_inc(decay_ready, 1)

            def split_piece(k):
                loads = sum(2 if m < BLOCKS else 1 for m in range(k % SLOTS, k + 1, SLOTS))
                dve.wait_ge(w_loaded[k % SLOTS], 16 * loads)
                if k < BLOCKS:
                    hi, lo = (w[:, k, :, :, :].rearrange("p g c d -> p (g c d)") for w in (w_h, w_l))
                else:
                    hi, lo = (w[:, k - BLOCKS, :] for w in (o_h, o_l))
                nc.vector.tensor_copy(hi, xt[:, k % SLOTS, :]).then_inc(w_split, 1)
                dve.wait_ge(w_split, 2 * k + 1)
                nc.vector.tensor_tensor(lo, xt[:, k % SLOTS, :], raw(hi), ALU.subtract).then_inc(w_split, 1)

            def convolve(it, s):
                n, b = it * STEPS + s, s % 2
                for tap in range(HALO):
                    for t in range(FT):
                        if tap == 0:
                            wait(dve, tapped, n * FT + t + 1)
                            if t == 0 and isinstance(it, int) and n == 0:
                                dve.wait_ge(clear, 4)
                        else:
                            wait(dve, convolved, (n * HALO + tap - 1) * FT + t + 1)
                        nc.vector.scalar_tensor_tensor(out=uc[b][:, t, :], in0=u[b][:, t, tap:tap + W],
                                                       scalar=column(par[:, tap, :], s, t), in1=uc[b][:, t, :],
                                                       op0=ALU.mult, op1=ALU.add).then_inc(convolved, 1)
                wait(dve, convolved, (n + 1) * HALO * FT)
                wait(dve, gates, n)
                nc.vector.tensor_copy(uh[:, :, :], uc[b][:, :, :]).then_inc(u_split, 1)
                wait(dve, u_split, 2 * n + 1)
                nc.vector.tensor_tensor(ul[:, :, :], uc[b][:, :, :], raw(uh[:, :, :]), ALU.subtract)\
                    .then_inc(u_split, 1)

            def remainder(it, s):
                n, b = it * STEPS + s, s % 2
                wait(dve, squared, n + 1)
                wait(dve, decayed, 2 * FT * (n + 1))
                nc.vector.scalar_tensor_tensor(out=r_[b][:, :, :], in0=q_[:, :, :], scalar=1.0, in1=r_[b][:, :, :],
                                               op0=ALU.add, op1=ALU.mult).then_inc(rest, 1)

            def scan(it, s):
                n, b = it * STEPS + s, s % 2
                wait(dve, rooted, n + 1)
                wait(dve, inputs, n + 1)
                nc.vector.tensor_tensor(i_[b][:, :, :], i_[b][:, :, :], r_[b][:, :, :], ALU.mult).then_inc(fed, 1)
                wait(dve, fed, n + 1)
                wait(dve, gated, n - 1)
                for t in range(FT):
                    nc.vector.tensor_tensor_scan(h_[b][:, t, :], a_[b][:, t, :], i_[b][:, t, :],
                                                 h_[b][:, t, W - 1:W], ALU.mult, ALU.add).then_inc(scanned, 1)

            def split_y(it, s):
                n, b = it * STEPS + s, s % 2
                wait(dve, gated, n + 1)
                wait(dve, merged, n)
                nc.vector.tensor_copy(yh[:, :, :], gate[b][:, :, :]).then_inc(y_split, 1)
                wait(dve, y_split, 2 * n + 1)
                nc.vector.tensor_tensor(yl[:, :, :], gate[b][:, :, :], raw(yh[:, :, :]), ALU.subtract)\
                    .then_inc(y_split, 1)

            def residual(it, s):
                if s % 2 == 0:
                    return
                wait(dve, merged, it * STEPS + s + 1)
                for k in slots(s):
                    n, b = it * SLOTS + k, k % 2
                    wait(dve, x_loaded[k], 16 * (it + 1))
                    row = xt[:, k, :].rearrange("p (h d) -> p h d", h=DH)
                    nc.vector.scalar_tensor_tensor(out=row, in0=row, scalar=ALPHA, in1=ops[b][:, :, :],
                                                   op0=ALU.mult, op1=ALU.add).then_inc(summed, 1)
                for k in slots(s):
                    n, b = it * SLOTS + k, k % 2
                    row = xt[:, k, :].rearrange("p (h d) -> p h d", h=DH)
                    wait(dve, summed, n + 1)
                    for h in range(DH):
                        nc.vector.bn_stats(stats[:, b, h, :], row[:, h, :]).then_inc(stat, 1)
                    wait(dve, stat, n * (DH + 2) + DH)
                    dve.sem_inc(gathered, 1)
                    nc.vector.bn_aggr(mean_var[:, b, :], stats[:, b, :, :]).then_inc(stat, 1)
                    wait(dve, stat, n * (DH + 2) + DH + 1)
                    nc.vector.tensor_scalar(mean_var[:, b, 1:2], mean_var[:, b, 1:2], LN_EPS, None, ALU.add)\
                        .then_inc(stat, 1)

            def normalize(it, s):
                if s % 2 == 0:
                    return
                for k in slots(s):
                    n, b = it * SLOTS + k, k % 2
                    wait(dve, dev_ready, n + 1)
                    nc.vector.reciprocal(rstd[:, b, 1:2], rstd[:, b, 0:1]).then_inc(inverted, 1)
                    wait(dve, inverted, n + 1)
                    nc.vector.tensor_scalar(xt[:, k, :], xt[:, k, :], mean_var[:, b, 0:1], rstd[:, b, 1:2],
                                            ALU.subtract, ALU.mult).then_inc(normed, 1)

            def step(it, s, begun):
                each(it, s, begun, 0, convolve)
                each(it, s, begun, 3, split_y)
                each(it, s, begun, 4, residual)
                if isinstance(it, int) and it == 0 and s < STEPS:
                    for k in range(2):
                        split_piece(BLOCKS + 2 * s + k)
                each(it, s, begun, 2, scan)
                each(it, s, begun, 4, normalize)
                each(it, s, begun, 1, remainder)

            for k in range(BLOCKS):
                split_piece(k)
            all_steps(dve, step)


_INS = ["x", "ln_g", "ln_b", "attn_w_in", "attn_b_f", "attn_w_out", "rnn_w_in", "rnn_conv_w", "rnn_conv_b",
        "rnn_w_a", "rnn_b_a", "rnn_w_i", "rnn_b_i", "rnn_lambda", "rnn_w_out"]


def build(nc, t, out):
    _, S, D = t["x"].shape
    x = t["x"].rearrange("b s d -> (b s) d")
    out = out.rearrange("b s d -> (b s) d")

    def dram(name, shape):
        return nc.dram_tensor(name, shape, F32, kind="Internal").ap()

    qs, ks, ys = (dram(n, (2, D, S)) for n in ("q_halves", "k_halves", "y_halves"))
    vs = dram("v_halves", (S, HEADS, 2 * HEAD_DIM))
    gs, us = dram("gate_path", (D, S)), dram("u_path", (D, S))
    cum = dram("forget_sums", (4, HEADS, S))
    x1 = dram("x1", (S, D))
    n = D // STRIP
    project(nc, "pa", x, t["attn_w_in"][0], [("split", 0, n, qs), ("split", D, n, ks), ("rows", 2 * D, n, vs),
                                              ("silu", 3 * D, n, gs)], t["attn_b_f"][0], cum)
    attend(nc, "at", qs, ks, vs, gs, cum, ys)
    merge(nc, "ma", ys, t["attn_w_out"][0], x, t["ln_g"][0], t["ln_b"][0], x1)
    project(nc, "pr", x1, t["rnn_w_in"][0], [("plain", 0, n, us), ("silu", D, n, gs)])
    recur(nc, "re", us, gs, t["rnn_conv_w"][0], t["rnn_conv_b"], t["rnn_w_a"][0], t["rnn_b_a"], t["rnn_w_i"][0],
          t["rnn_b_i"], t["rnn_lambda"], t["rnn_w_out"][0], x1, t["ln_g"][1], t["ln_b"][1], out)


def kernel(**inputs):
    import numpy as _np
    import concourse.bacc as _bacc
    from concourse import mybir as _mybir
    from concourse.bass_utils import run_bass_kernel_spmd as _run

    nc = _bacc.Bacc("TRN2", target_bir_lowering=False, num_devices=1)
    arrays, args = {}, {}
    for name in _INS:
        v = _np.ascontiguousarray(inputs[name])
        arrays[f"in_{name}"] = v
        args[name] = nc.dram_tensor(f"in_{name}", v.shape, _mybir.dt.from_np(v.dtype), kind="ExternalInput").ap()
    out = nc.dram_tensor("out", inputs["x"].shape, F32, kind="ExternalOutput").ap()
    build(nc, args, out)
    r = _run(nc, [arrays], core_ids=[0])
    return r.results[0]["out"]
```
